# Optimizing a Trainium2 kernel written in Bass

```python
import math
import jax, jax.numpy as jnp
from jax import lax
import numpy as np

D_MODEL = 1024
BATCH = 1
SEQ = 256
DEPTH = 2

MIX_W = D_MODEL
N_MIXERS = 4
GROUP_W = MIX_W // N_MIXERS
NORM_EPS = 1e-6

A_HEADS = 4
A_HEAD_DIM = GROUP_W // A_HEADS
DILATED_PATTERNS = ((128, 1), (512, 4), (2048, 16))
N_BUCKETS = 32
REL_MAX_DIST = 2048

CONV_WIDTH = 31
CONV_GROUPS = 4
CONV_LN_EPS = 1e-5

RWKV_HEADS = 4
RWKV_HEAD_DIM = GROUP_W // RWKV_HEADS
RWKV_DECAY_LORA = 32
RWKV_AAA_LORA = 32
RWKV_GATE_LORA = 64
RWKV_LN_EPS = 64e-5

GLA_HEADS = 4
GLA_KEY_DIM = GROUP_W // 2 // GLA_HEADS
GLA_VAL_DIM = GROUP_W // GLA_HEADS
GLA_GATE_LORA = 16
GLA_TAU = 16.0
GLA_CHUNK = 64

D_FF = 2816
N_EXPERTS = 8
TOP_K = 2
MOE_BLOCK = 256
N_DENSE = (DEPTH + 1) // 2
N_MOE = DEPTH // 2

SPLIT_A = (GROUP_W, GROUP_W, GROUP_W)
SPLIT_B = (GROUP_W, GROUP_W)
SPLIT_C = (GROUP_W, GROUP_W, GROUP_W, RWKV_DECAY_LORA, RWKV_AAA_LORA, RWKV_GATE_LORA)
SPLIT_D = (GLA_HEADS * GLA_KEY_DIM, GLA_HEADS * GLA_KEY_DIM, GROUP_W, GLA_GATE_LORA, GROUP_W)
SEGMENTS = (sum(SPLIT_A), sum(SPLIT_B), sum(SPLIT_C), sum(SPLIT_D))
C_IN_W = sum(SPLIT_C)
IN_W = sum(SEGMENTS)

kernel_name = 'hybrid_dilated_conv_rwkv7_gla_moe'

def _split(z, sizes):
    return jnp.split(z, np.cumsum(sizes)[:-1].tolist(), axis=-1)

def _rms_norm(x, g, eps=NORM_EPS):
    xf = x.astype(jnp.float32)
    return xf * lax.rsqrt(jnp.mean(xf * xf, axis=-1, keepdims=True) + eps) * g.astype(jnp.float32)

def _layer_norm(x, eps):
    mu = jnp.mean(x, axis=-1, keepdims=True)
    xc = x - mu
    return xc * lax.rsqrt(jnp.mean(xc * xc, axis=-1, keepdims=True) + eps)

def _t5_bucket(dist):
    max_exact = N_BUCKETS // 2
    n = np.maximum(dist, 0)
    large = max_exact + (np.log(np.maximum(n, 1) / max_exact) / math.log(REL_MAX_DIST / max_exact)
                         * (N_BUCKETS - max_exact)).astype(np.int32)
    large = np.minimum(large, N_BUCKETS - 1)
    return np.where(n < max_exact, n, large).astype(np.int32)

def _dilated_branch(q, k, v, rel_bias, window, dilation):
    B, S, H, E = q.shape
    W = window // dilation
    L = S // dilation
    nb = -(-L // W)
    Lp = nb * W

    def to_blocks(z):
        z = z.reshape(B, L, dilation, H, E).transpose(0, 2, 3, 1, 4)
        z = jnp.pad(z, ((0, 0), (0, 0), (0, 0), (0, Lp - L), (0, 0)))
        return z.reshape(B, dilation, H, nb, W, E)

    def with_prev(z):
        prev = jnp.pad(z[:, :, :, :-1], ((0, 0), (0, 0), (0, 0), (1, 0), (0, 0), (0, 0)))
        return jnp.concatenate([prev, z], axis=4)

    qb = to_blocks(q)
    kb = with_prev(to_blocks(k))
    vb = with_prev(to_blocks(v))
    s = jnp.einsum('bdhnqe,bdhnke->bdhnqk', qb, kb)

    delta = np.arange(W)[:, None] + W - np.arange(2 * W)[None, :]
    band = (delta >= 0) & (delta <= W)
    bucket = _t5_bucket(np.clip(delta, 0, W) * dilation)
    bias = jnp.transpose(rel_bias.astype(jnp.float32)[bucket], (2, 0, 1))
    key_ok = ~((np.arange(nb)[:, None] == 0) & (np.arange(2 * W)[None, :] < W))
    mask = band[None] & key_ok[:, None, :]

    s = jnp.where(mask, s + bias[:, None], -jnp.inf)
    m = jnp.max(s, axis=-1, keepdims=True)
    p = jnp.exp(s - m)
    den = jnp.sum(p, axis=-1, keepdims=True)
    o = jnp.einsum('bdhnqk,bdhnke->bdhnqe', p, vb) / den
    lse = (m + jnp.log(den))[..., 0]
    o = o.reshape(B, dilation, H, Lp, E)[:, :, :, :L].transpose(0, 3, 1, 2, 4).reshape(B, S, H, E)
    lse = lse.reshape(B, dilation, H, Lp)[:, :, :, :L].transpose(0, 3, 1, 2).reshape(B, S, H)
    return o, lse

def _mixer_dilated(za, q_g, k_g, rel_bias):
    B, S, _ = za.shape
    qa, ka, va = _split(za, SPLIT_A)
    shp = (B, S, A_HEADS, A_HEAD_DIM)
    q = _rms_norm(qa.reshape(shp), q_g) * (A_HEAD_DIM ** -0.5)
    k = _rms_norm(ka.reshape(shp), k_g)
    v = va.reshape(shp).astype(jnp.float32)
    outs, lses = [], []
    for window, dilation in DILATED_PATTERNS:
        o, lse = _dilated_branch(q, k, v, rel_bias, window, dilation)
        outs.append(o)
        lses.append(lse)
    wts = jax.nn.softmax(jnp.stack(lses, 0), axis=0)
    o = jnp.sum(wts[..., None] * jnp.stack(outs, 0), axis=0)
    return o.reshape(B, S, GROUP_W)

def _mixer_conv(zb, conv_w, conv_b, ln_g, ln_b):
    B, S, _ = zb.shape
    u, gate = _split(zb.astype(jnp.float32), SPLIT_B)
    h = u * jax.nn.sigmoid(gate)
    h = lax.conv_general_dilated(h, conv_w.astype(jnp.float32)[:, None, :], window_strides=(1,),
                                 padding=[(CONV_WIDTH - 1, 0)], dimension_numbers=('NWC', 'WIO', 'NWC'),
                                 feature_group_count=GROUP_W) + conv_b.astype(jnp.float32)
    h = _layer_norm(h.reshape(B, S, CONV_GROUPS, GROUP_W // CONV_GROUPS), CONV_LN_EPS).reshape(B, S, GROUP_W)
    h = h * ln_g.astype(jnp.float32) + ln_b.astype(jnp.float32)
    return jax.nn.silu(h)

def _mixer_rwkv7(zc, mu, w0, w2, a0, a2, g2, k_k, k_a, r_k, ln_g, ln_b):
    B, S, _ = zc.shape
    f32 = jnp.float32
    zc = zc.astype(f32)
    prev = jnp.pad(zc[:, :-1], ((0, 0), (1, 0), (0, 0)))
    zc = zc + (prev - zc) * mu.astype(f32)
    r, k, v, wd, ad, gd = _split(zc, SPLIT_C)
    w_log = -jax.nn.softplus(-(w0.astype(f32) + jnp.tanh(wd) @ w2.astype(f32))) - 0.5
    decay = jnp.exp(-jnp.exp(w_log))
    a = jax.nn.sigmoid(a0.astype(f32) + ad @ a2.astype(f32))
    g = jax.nn.sigmoid(gd) @ g2.astype(f32)

    def heads(t):
        return t.reshape(B, S, RWKV_HEADS, RWKV_HEAD_DIM)

    kk = heads(k * k_k.astype(f32))
    kk = kk / jnp.maximum(jnp.linalg.norm(kk, axis=-1, keepdims=True), 1e-12)
    k = heads(k * (1.0 + (a - 1.0) * k_a.astype(f32)))
    r, v, decay, a = heads(r), heads(v), heads(decay), heads(a)

    def step(state, inp):
        r_t, w_t, k_t, v_t, kk_t, a_t = inp
        sa = jnp.einsum('bhvk,bhk->bhv', state, -kk_t)
        state = (state * w_t[:, :, None, :] + sa[..., None] * (kk_t * a_t)[:, :, None, :]
                 + v_t[..., None] * k_t[:, :, None, :])
        return state, jnp.einsum('bhvk,bhk->bhv', state, r_t)

    xs = tuple(jnp.moveaxis(t, 1, 0) for t in (r, decay, k, v, kk, a))
    s0 = jnp.zeros((B, RWKV_HEADS, RWKV_HEAD_DIM, RWKV_HEAD_DIM), f32)
    _, out = lax.scan(step, s0, xs)
    out = jnp.moveaxis(out, 0, 1)
    out = _layer_norm(out, RWKV_LN_EPS).reshape(B, S, GROUP_W) * ln_g.astype(f32) + ln_b.astype(f32)
    bonus = jnp.sum(r * k * r_k.astype(f32), axis=-1, keepdims=True) * v
    out = out + bonus.reshape(B, S, GROUP_W)
    return out * g

def _gla_chunked(q, k, v, gk):
    B, S, H, K = q.shape
    V = v.shape[-1]
    n = S // GLA_CHUNK

    def chunks(z):
        return z.reshape(B, n, GLA_CHUNK, H, z.shape[-1]).transpose(0, 3, 1, 2, 4)

    q, k, v, gk = chunks(q), chunks(k), chunks(v), chunks(gk)
    b = jnp.cumsum(gk, axis=3)
    q_d = q * jnp.exp(b)
    k_d = k * jnp.exp(-b)
    causal = np.tril(np.ones((GLA_CHUNK, GLA_CHUNK), dtype=bool))
    att = jnp.where(causal, jnp.einsum('bhncd,bhnjd->bhncj', q_d, k_d), 0.0)
    o = jnp.einsum('bhncj,bhnje->bhnce', att, v)
    b_last = b[:, :, :, -1:]
    contrib = jnp.einsum('bhncd,bhnce->bhnde', k * jnp.exp(b_last - b), v)
    chunk_decay = jnp.exp(b_last[:, :, :, 0])

    def step(state, inp):
        dec, con = inp
        return dec[..., None] * state + con, state

    _, s_prev = lax.scan(step, jnp.zeros((B, H, K, V), jnp.float32),
                         (jnp.moveaxis(chunk_decay, 2, 0), jnp.moveaxis(contrib, 2, 0)))
    s_prev = jnp.moveaxis(s_prev, 0, 2)
    o = o + jnp.einsum('bhncd,bhnde->bhnce', q_d, s_prev)
    return o.transpose(0, 2, 3, 1, 4).reshape(B, S, H, V)

def _mixer_gla(zd, g2, gb, norm_g):
    B, S, _ = zd.shape
    f32 = jnp.float32
    qd, kd, vd, gd, og = _split(zd.astype(f32), SPLIT_D)
    q = qd.reshape(B, S, GLA_HEADS, GLA_KEY_DIM) * (GLA_KEY_DIM ** -0.5)
    k = kd.reshape(B, S, GLA_HEADS, GLA_KEY_DIM)
    v = vd.reshape(B, S, GLA_HEADS, GLA_VAL_DIM)
    gk = jax.nn.log_sigmoid(gd @ g2.astype(f32) + gb.astype(f32)) / GLA_TAU
    o = _gla_chunked(q, k, v, gk.reshape(B, S, GLA_HEADS, GLA_KEY_DIM))
    o = _rms_norm(o, norm_g) * jax.nn.silu(og.reshape(B, S, GLA_HEADS, GLA_VAL_DIM))
    return o.reshape(B, S, GROUP_W)

def _swiglu(x, wg, wu, wd):
    return (jax.nn.silu(x @ wg) * (x @ wu)) @ wd

def _moe(xn, router, wg, wu, wd):
    B, S, D = xn.shape
    T = B * S
    xt = xn.reshape(T, D)
    logits = (xt @ router).astype(jnp.float32)
    top_logits, top_idx = lax.top_k(logits, TOP_K)
    gates = jax.nn.softmax(top_logits, axis=-1)
    n_assign = T * TOP_K
    exp_id = top_idx.reshape(-1).astype(jnp.int32)
    tok_id = jnp.repeat(jnp.arange(T, dtype=jnp.int32), TOP_K)
    order = jnp.argsort(exp_id)
    e_sorted, t_sorted, g_sorted = exp_id[order], tok_id[order], gates.reshape(-1)[order]
    counts = jax.ops.segment_sum(jnp.ones_like(exp_id), exp_id, num_segments=N_EXPERTS)
    starts = jnp.cumsum(counts) - counts
    padded = (counts + MOE_BLOCK - 1) // MOE_BLOCK * MOE_BLOCK
    pends = jnp.cumsum(padded)
    pstarts = pends - padded
    dest = pstarts[e_sorted] + jnp.arange(n_assign, dtype=jnp.int32) - starts[e_sorted]
    n_blocks = -(-n_assign // MOE_BLOCK) + N_EXPERTS
    buf = jnp.zeros((n_blocks * MOE_BLOCK, D), xt.dtype).at[dest].set(xt[t_sorted])
    block_expert = jnp.minimum(jnp.searchsorted(pends, jnp.arange(n_blocks) * MOE_BLOCK, side='right'),
                               N_EXPERTS - 1)

    def run_block(args):
        xb, e = args
        return _swiglu(xb, wg[e], wu[e], wd[e])

    yb = lax.map(run_block, (buf.reshape(n_blocks, MOE_BLOCK, D), block_expert))
    y_sorted = yb.reshape(-1, D)[dest].astype(jnp.float32) * g_sorted[:, None]
    y = jnp.zeros((T, D), jnp.float32).at[t_sorted].add(y_sorted)
    return y.reshape(B, S, D)

def setup_inputs(seed: int = 0) -> dict:
    key = jax.random.key(seed)
    ks = iter(jax.random.split(key, 40))
    f32 = jnp.float32

    def nrm(shape, scale):
        return scale * jax.random.normal(next(ks), shape, f32)

    def gain(shape):
        return 1.0 + nrm(shape, 0.1)

    def unif(shape, lo, hi):
        return jax.random.uniform(next(ks), shape, f32, lo, hi)

    return {
        'x': nrm((BATCH, SEQ, D_MODEL), 1.0),
        'rel_bias': nrm((N_BUCKETS, A_HEADS), 0.5),
        'mix_norm_g': gain((DEPTH, D_MODEL)),
        'w_in': nrm((DEPTH, D_MODEL, IN_W), D_MODEL ** -0.5),
        'w_out': nrm((DEPTH, MIX_W, D_MODEL), MIX_W ** -0.5),
        'ffn_norm_g': gain((DEPTH, D_MODEL)),
        'attn_q_norm_g': gain((DEPTH, A_HEAD_DIM)),
        'attn_k_norm_g': gain((DEPTH, A_HEAD_DIM)),
        'conv_w': nrm((DEPTH, CONV_WIDTH, GROUP_W), CONV_WIDTH ** -0.5),
        'conv_b': nrm((DEPTH, GROUP_W), 0.02),
        'conv_ln_g': gain((DEPTH, GROUP_W)),
        'conv_ln_b': nrm((DEPTH, GROUP_W), 0.02),
        'rwkv_mu': unif((DEPTH, C_IN_W), 0.0, 1.0),
        'rwkv_w0': unif((DEPTH, GROUP_W), -5.0, 1.0),
        'rwkv_w2': nrm((DEPTH, RWKV_DECAY_LORA, GROUP_W), 0.1),
        'rwkv_a0': nrm((DEPTH, GROUP_W), 0.5),
        'rwkv_a2': nrm((DEPTH, RWKV_AAA_LORA, GROUP_W), 0.5 * RWKV_AAA_LORA ** -0.5),
        'rwkv_g2': nrm((DEPTH, RWKV_GATE_LORA, GROUP_W), RWKV_GATE_LORA ** -0.5),
        'rwkv_k_k': 0.85 + nrm((DEPTH, GROUP_W), 0.1),
        'rwkv_k_a': gain((DEPTH, GROUP_W)),
        'rwkv_r_k': nrm((DEPTH, RWKV_HEADS, RWKV_HEAD_DIM), 0.1),
        'rwkv_ln_g': gain((DEPTH, GROUP_W)),
        'rwkv_ln_b': nrm((DEPTH, GROUP_W), 0.02),
        'gla_g2': nrm((DEPTH, GLA_GATE_LORA, GLA_HEADS * GLA_KEY_DIM), GLA_GATE_LORA ** -0.5),
        'gla_gb': nrm((DEPTH, GLA_HEADS * GLA_KEY_DIM), 0.5),
        'gla_norm_g': gain((DEPTH, GLA_VAL_DIM)),
        'ffn_wg': nrm((N_DENSE, D_MODEL, D_FF), D_MODEL ** -0.5),
        'ffn_wu': nrm((N_DENSE, D_MODEL, D_FF), D_MODEL ** -0.5),
        'ffn_wd': nrm((N_DENSE, D_FF, D_MODEL), D_FF ** -0.5),
        'moe_router': nrm((N_MOE, D_MODEL, N_EXPERTS), D_MODEL ** -0.5),
        'moe_wg': nrm((N_MOE, N_EXPERTS, D_MODEL, D_FF), D_MODEL ** -0.5),
        'moe_wu': nrm((N_MOE, N_EXPERTS, D_MODEL, D_FF), D_MODEL ** -0.5),
        'moe_wd': nrm((N_MOE, N_EXPERTS, D_FF, D_MODEL), D_FF ** -0.5),
    }

def reference(x, rel_bias, mix_norm_g, w_in, w_out, ffn_norm_g, attn_q_norm_g, attn_k_norm_g,
              conv_w, conv_b, conv_ln_g, conv_ln_b, rwkv_mu, rwkv_w0, rwkv_w2, rwkv_a0, rwkv_a2,
              rwkv_g2, rwkv_k_k, rwkv_k_a, rwkv_r_k, rwkv_ln_g, rwkv_ln_b, gla_g2, gla_gb, gla_norm_g,
              ffn_wg, ffn_wu, ffn_wd, moe_router, moe_wg, moe_wu, moe_wd):
    h = x
    for layer in range(DEPTH):
        xn = _rms_norm(h, mix_norm_g[layer]).astype(h.dtype)
        z = xn @ w_in[layer]
        za, zb, zc, zd = _split(z, SEGMENTS)
        ya = _mixer_dilated(za, attn_q_norm_g[layer], attn_k_norm_g[layer], rel_bias)
        yb = _mixer_conv(zb, conv_w[layer], conv_b[layer], conv_ln_g[layer], conv_ln_b[layer])
        yc = _mixer_rwkv7(zc, rwkv_mu[layer], rwkv_w0[layer], rwkv_w2[layer], rwkv_a0[layer], rwkv_a2[layer],
                          rwkv_g2[layer], rwkv_k_k[layer], rwkv_k_a[layer], rwkv_r_k[layer],
                          rwkv_ln_g[layer], rwkv_ln_b[layer])
        yd = _mixer_gla(zd, gla_g2[layer], gla_gb[layer], gla_norm_g[layer])
        y = jnp.concatenate([ya, yb, yc, yd], axis=-1).astype(h.dtype)
        h = h + (y @ w_out[layer]).astype(h.dtype)
        hn = _rms_norm(h, ffn_norm_g[layer]).astype(h.dtype)
        i = layer // 2
        if layer % 2 == 0:
            f = _swiglu(hn, ffn_wg[i], ffn_wu[i], ffn_wd[i])
        else:
            f = _moe(hn, moe_router[i], moe_wg[i], moe_wu[i], moe_wd[i])
        h = h + f.astype(h.dtype)
    return h


_drawn_inputs = setup_inputs


def setup_inputs(seed=0):
    import zlib

    import numpy as np

    out = dict(_drawn_inputs(seed))
    spreads = {}
    factors = {'conv_ln_b': 3.347, 'rwkv_ln_b': 3.778}
    for name, (base, spread) in spreads.items():
        noise = np.random.default_rng([zlib.crc32(name.encode()), seed]).standard_normal(out[name].shape)
        drawn = base * np.exp(spread * noise) if base else spread * noise
        out[name] = __import__('jax').numpy.asarray(drawn.astype(out[name].dtype))
    for name, factor in factors.items():
        out[name] = (out[name] * factor).astype(out[name].dtype)
    return out
```

```python
from contextlib import ExitStack
import math

import numpy as np
import concourse.bass as bass
import concourse.mybir as mybir

ALU = mybir.AluOpType
ACT = mybir.ActivationFunctionType
AX_X = mybir.AxisListType.X
F32 = mybir.dt.float32
F32R = mybir.dt.float32r
U32 = mybir.dt.uint32
I32 = mybir.dt.int32

P = 128
D = 1024
S = 256
LAYERS = 2
T = S // P
KD = D // P
GROUP = 256
PAIRS = GROUP // P
HD = 64
CW = 31
CHUNK = 64
NCH = S // CHUNK
FF = 2816
FB = FF // P
NE = 8
EPS = 1e-6
LEVELS = 6
KAPPA = math.exp(-0.5)

UC = 1024
RAW = 3
RING = 6
Z_UNITS = 24
O_UNITS = 8
F_UNITS = 3 * FB
LAYER_UNITS = Z_UNITS + O_UNITS
DENSE_AT = LAYER_UNITS
LAYER1_AT = DENSE_AT + F_UNITS
MOE_AT = LAYER1_AT + LAYER_UNITS
MAIN_UNITS = MOE_AT + NE * F_UNITS + 2
AGAIN_AT = MAIN_UNITS
assert F_UNITS % RING == 0 and F_UNITS % RAW == 0

_A, _B, _C, _D = 0, 768, 1280, 2176
Z_COLS = [(_C + 128 * i, 128) for i in range(7)]
Z_COLS += [(_D, 128), (_D + 128, 128), (_D + 256, 128), (_D + 384, 128), (_D + 512, 16),
           (_D + 528, 128), (_D + 656, 128)]
Z_COLS += [(_A + 128 * i, 128) for i in range(6)]
Z_COLS += [(_B + 128 * i, 128) for i in range(4)]
assert len(Z_COLS) == Z_UNITS
UC0, UD0, UA0, UB0 = 0, 7, 14, 20

VEC = {}
for _name, _n in (("mix_g", 8), ("ffn_g", 8), ("q_g", 1), ("k_g0", 1), ("k_g1", 1), ("conv_w", 2 * CW),
                  ("conv_b", 2), ("conv_g", 2), ("conv_lb", 2), ("mu", 7), ("w0", 2), ("a0", 2), ("k_k", 2),
                  ("k_a", 2), ("r_k", 2), ("ln_g", 2), ("ln_b", 2), ("gb", 1), ("gn_g", 1)):
    VEC[_name] = (sum(n for _, n in VEC.values()), _n)
NV = sum(n for _, n in VEC.values())

CON = {}
for _name, _n in (("ident", P), ("blk", P), ("lvl", LEVELS * P), ("mask_g", 4 * P), ("logm", 3 * P),
                  ("upper", P), ("ones", P), ("iota", 2 * P), ("restart", S), ("iota8", 8),
                  ("head32", 4), ("eps", 3), ("bd_d", 2 * P), ("buckets", 3 * P)):
    CON[_name] = (sum(n for _, n in CON.values()), _n)
NC_ = sum(n for _, n in CON.values())
NCON = CON["buckets"][0]

NEG = -1e30


def t5_bucket(dist):
    n = np.maximum(dist, 0)
    large = 16 + (np.log(np.maximum(n, 1) / 16) / math.log(2048 / 16) * 16).astype(np.int32)
    return np.where(n < 16, n, np.minimum(large, 31)).astype(np.int32)


def constants():
    c = np.zeros((P, NC_), np.float32)

    def put(name, a):
        o, n = CON[name]
        c[:a.shape[0], o:o + n] = a.reshape(a.shape[0], -1)

    r, q = np.arange(P)[:, None], np.arange(P)[None, :]
    put("ident", np.eye(P, dtype=np.float32))
    put("blk", (r // HD == q // HD) / HD)
    lv = [(r // (2 << l) == q // (2 << l)) & ((r >> l) % 2 == 1) & ((q >> l) % 2 == 0) for l in range(LEVELS)]
    put("lvl", np.stack(lv, 1).astype(np.float32))
    same = r // CHUNK == q // CHUNK
    su, iu = same & (r < q), same & (r <= q)
    put("mask_g", np.stack([su, iu, su, iu], 1).astype(np.float32))
    cols = []
    for t0, j0 in ((0, 0), (128, 0), (128, 128)):
        d = (t0 + r) - (j0 + q)
        m = ((d >= 0) & (d <= 128)).astype(int) + ((d >= 0) & (d % 4 == 0)) + ((d >= 0) & (d % 16 == 0))
        cols.append(np.where(m > 0, np.log(np.maximum(m, 1)), NEG))
    put("logm", np.stack(cols, 1).astype(np.float32))
    put("upper", (r < q).astype(np.float32))
    put("ones", np.ones((P, P), np.float32))
    put("iota", np.broadcast_to(np.arange(2 * P), (P, 2 * P)))
    put("restart", np.broadcast_to((np.arange(S) % CHUNK != 0), (P, S)).astype(np.float32))
    put("iota8", np.broadcast_to(np.arange(8), (P, 8)))
    put("eps", np.broadcast_to(np.array([EPS, 64e-5, 1e-5]), (P, 3)))
    put("head32", (r // 32 == np.arange(4)[None, :]).astype(np.float32))
    put("bd_d", (r // 32 == np.arange(2 * P)[None, :] // HD).astype(np.float32))
    y = np.arange(3 * P)[None, :]
    dist = (S - 1) - y
    put("buckets", ((np.arange(32)[:, None] == t5_bucket(dist)) & (dist >= 0)).astype(np.float32))
    return c


class Chain:

    def __init__(self, eng, sem):
        self.eng, self.sem, self.n, self.base, self.reg, self.per = eng, sem, 0, 0, None, 0

    def loop(self, reg, per):
        self.base, self.n, self.reg, self.per = self.n, 0, reg, per

    def end_loop(self, times):
        assert self.n == self.per, (self.n, self.per)
        self.n, self.reg = self.base + self.per * times, None

    def value(self):
        return self.n if self.reg is None else self.reg * self.per + (self.base + self.n)

    def __call__(self, ins):
        self.n += 1
        ins.then_inc(self.sem, 1)
        self.eng.wait_ge(self.sem, self.value())


class Area:

    def __init__(self, tensor, at=0, end=None):
        self.tensor, self.at, self.end = tensor, at, end or tensor.shape[1]

    def __call__(self, *shape):
        n = int(np.prod(shape))
        v = self.tensor[:, self.at:self.at + n]
        self.at += n
        assert self.at <= self.end, (self.at, self.end)
        if len(shape) > 1:
            names = "abcde"[:len(shape)]
            sizes = {k: s for k, s in zip(names[1:], shape[1:])}
            v = v.rearrange("p (" + " ".join(names) + ") -> p " + " ".join(names), **sizes)
        return v


def build(nc, x, cons, vecs, lora, gla2, router, relb, wst, out, stop=99):
    ctx = ExitStack()
    with ctx:
        def sb(name, shape, dt=F32):
            return ctx.enter_context(nc.sbuf_tensor(name, shape, dt))

        sems = {}

        def sem(name):
            if name not in sems:
                sems[name] = ctx.enter_context(nc.semaphore(name))
            return sems[name]

        bank = [ctx.enter_context(nc.psum_tensor(f"bank{i}", [P, 512], F32)) for i in range(8)]

        h = sb("h", [P, T, D])
        xsq = sb("xsq", [P, T * D])
        xnf = sb("xnf", [P, KD, S])
        xhi = sb("xhi", [P, KD, S], F32R)
        xlo = sb("xlo", [P, KD, S], F32R)
        raw = sb("raw", [P, RAW, UC])
        whi = sb("whi", [P, RING, UC], F32R)
        wlo = sb("wlo", [P, RING, UC], F32R)
        con = sb("con", [P, NCON])
        vec = sb("vec", [P, LAYERS, NV])
        lor = sb("lor", [P, LAYERS, 3, GROUP])
        g2s = sb("g2s", [16, LAYERS, P])
        rou = sb("rou", [P, KD, NE])
        rel = sb("rel", [32, 4, P])
        bias0 = sb("bias0", [P, 4, P])
        bias1 = sb("bias1", [P, 4, S])
        small = sb("small", [P, 64])
        idx = sb("idx", [P, T, 8], U32)
        over = sb("over", [P, 1], I32)
        hthi = sb("hthi", [P, 2, P], F32R)
        htlo = sb("htlo", [P, 2, P], F32R)
        arena = sb("arena", [P, 18256])
        ext_dram = nc.dram_tensor("ext_dram", [P, 4, 3 * P], F32, kind="Internal").ap()
        xs = xsq[:, :].rearrange("p (t d) -> p t d", t=T)
        yT = xnf
        ssq, rstd, cnt = small[:, 0:2], small[:, 2:4], small[:, 4:6]
        negm, den, rden = small[:, 8:16], small[:, 16:24], small[:, 24:32]

        def C(name, a=0, b=None):
            o, n = CON[name]
            return con[:, o + a:o + (n if b is None else b)]

        def V(L, name, i=0, n=1):
            return vec[:, L, VEC[name][0] + i:VEC[name][0] + i + n]

        blk, ident = C("blk"), C("ident")

        def over4(a):
            return a.unsqueeze(1).to_broadcast([P, 4, P])

        ax = Area(xsq)
        qkA, vA, gB = ax(4, S), ax(T, GROUP), ax(2, S)
        ar = Area(arena)
        zC = ar(7, S + 1)
        X, BVs = Area(arena)(8, P), Area(arena, 8 * P)(T, PAIRS, 2, HD)
        XA = Area(arena)(T * PAIRS, P)
        qkD, vD, gdD, ogD = ar(2, S), ar(T, GROUP), ar(S), ar(2, S)
        uB, hB = ar(2, S), ar(2, S + CW - 1)
        free_at = ar.at
        zs = ar(7, S)
        st_at = ar.at
        lin, sgw, sga = ar(S), ar(PAIRS, S), ar(PAIRS, S)
        ST = Area(arena, st_at)(NCH, PAIRS, P)
        gC, bonus = ar(PAIRS, S), ar(PAIRS, S)
        cum_at = ar.at
        cum, cinv, kkn, knew = ar(PAIRS, S), ar(PAIRS, S), ar(PAIRS, S), ar(PAIRS, S)
        ca = Area(arena, cum_at)
        khtok, betok, Ws, Us = ca(T, GROUP), ca(T, GROUP), ca(T, PAIRS, P), ca(T, PAIRS, P)
        alr = ar(2, PAIRS, S)
        sq_at = ar.at
        sq = ar(PAIRS, S)
        altok = Area(arena, sq_at)(T, GROUP)
        cend = ar(PAIRS, NCH)
        vtok = ar(T, GROUP)
        mats = ar(8, 4, P)
        XT = ar(8, P)
        stc = ar(PAIRS, P)
        yC = sq
        yc2 = Area(arena, cum_at)(PAIRS, S)

        ad = Area(arena, free_at)
        els, cumd, lsg, dl, eb, enb = ad(S), ad(S), ad(S), ad(S), ad(S), ad(S)
        qd, kd, kl, qx = ad(S), ad(S), ad(S), ad(4, S)
        attD, kltok, SD, cm = ad(T, 4, P), ad(T, P), ad(NCH, GROUP), ad(GROUP)
        oD, sqD, rsD, sgo = ad(PAIRS, S), ad(PAIRS, S), ad(PAIRS, S), ad(PAIRS, S)
        aa = Area(arena, ad.at)
        sqA, qn, kx = aa(4, S), aa(PAIRS, S), aa(2, PAIRS, S)
        aa2 = Area(arena, free_at)
        s0, s1, pt = aa2(4, P), aa2(4, S), aa2(12, P)
        ab = Area(arena, free_at + 4096)
        sgb, acc, xcB, sqB = ab(2, S), ab(2, S), ab(2, S), ab(2, S)

        am = Area(arena)
        xgf, sel, selg, selgt = am(KD, P), am(T, P), am(T, P), am(T, P)
        sg, hm, ysb = am(2, P), am(2, P), am(D)
        rkm, gat = am(T, NE + 1), am(T, NE)
        lg, top, idxf, e1, e2, mk = am(T, NE), am(T, 8), am(T, 8), am(T, NE), am(T, NE), am(T, NE)
        dif, ga, gb_ = am(T, 1), am(T, 1), am(T, 1)
        aext = Area(arena)
        bkt, ext = aext(3 * P), aext(4, 3 * P)

        def unit(L, u):
            return (0 if L == 0 else LAYER1_AT) + u

        def z_at(u):
            if u < UD0:
                return zC[:, u, 1:S + 1], False
            if u < UA0:
                v = u - UD0
                return [qkD[:, 0, :], qkD[:, 1, :], vD[:, :, 0:P], vD[:, :, P:2 * P], gdD, ogD[:, 0, :],
                        ogD[:, 1, :]][v], v in (2, 3)
            if u < UB0:
                v = u - UA0
                return (qkA[:, v, :], False) if v < 4 else (vA[:, :, (v - 4) * P:(v - 3) * P], True)
            v = u - UB0
            return [uB, gB][v // 2][:, v % 2, :], False

        def at(reg, per, v):
            return v if reg is None else reg * per + v

        def hi(e, n, reg=None):
            e.wait_ge(sem(f"raw_in{n % RAW}"), at(reg, 16 * F_UNITS // RAW, 16 * (n // RAW + 1)))
            if n >= RING:
                e.wait_ge(sem("w_used"), at(reg, F_UNITS, n - RING + 1))
            e.activation(whi[:, n % RING, :], raw[:, n % RAW, :], ACT.Copy).then_inc(sem("w_high"), 1)

        def lo(e, n, reg=None):
            e.wait_ge(sem("w_high"), at(reg, F_UNITS, n + 1))
            e.tensor_tensor(wlo[:, n % RING, :], raw[:, n % RAW, :], whi[:, n % RING, :].bitcast(F32),
                            ALU.subtract).then_inc(sem("w_split"), 1)

        def gu_unit(b):
            return 0 if b == 0 else 2 + 3 * (b - 1)

        def wd_unit(b):
            return 2 + 3 * b + (2 if b < FB - 1 else 0)

        def wait_gate_up(e, j, first=None, reg=None):
            if first is not None:
                b = (j - 2 * FB) % FB
                e.wait_ge(sem("w_used"), at(reg, F_UNITS, first + gu_unit(b) + 2))
            elif j % 2 == 0:
                e.wait_ge(sem("gu"), j // 2 + 1)
            else:
                e.wait_ge(sem("w_used"), DENSE_AT + 3 * (j // 2) + 2)

        def wait_down(e, j, first=None, reg=None, before=0):
            if first is not None:
                b = (j - 2 * FB) % FB - before
                n = first + wd_unit(b % FB) + 1 - (F_UNITS if b < 0 else 0)
                e.wait_ge(sem("w_used"), at(reg, F_UNITS, n))
            elif (j - before) % 2 == 0:
                e.wait_ge(sem("down"), (j - before) // 2 + 1)
            else:
                e.wait_ge(sem("w_used"), DENSE_AT + 3 * ((j - before) // 2) + 3)

        block = ctx.enter_context(nc.Block())

        @block.sync
        def _(sp):
            sp.dma_start(h[:], x.rearrange("(t p) d -> p t d", p=P)).then_inc(sem("x_in"), 16)
            for n in range(RAW):
                sp.dma_start(raw[:, n, :], wst[n]).then_inc(sem(f"raw_in{n}"), 16)
            o, n = CON["buckets"]
            sp.dma_start(bkt, cons[:, o:o + n]).then_inc(sem("ext_in"), 16)
            sp.dma_start(rel[:], relb).then_inc(sem("ext_in"), 16)
            sp.dma_start(con[:], cons[:, 0:NCON]).then_inc(sem("con_in"), 16)
            sp.dma_start(vec[:], vecs).then_inc(sem("con_in"), 16)
            sp.dma_start(lor[:], lora).then_inc(sem("con_in"), 16)
            sp.dma_start(g2s[:], gla2).then_inc(sem("con_in"), 16)
            sp.dma_start(rou[:], router).then_inc(sem("con_in"), 16)
            sp.wait_ge(sem("ext_sb"), 4)
            sp.dma_start(ext_dram, ext).then_inc(sem("ext_out"), 16)
            sp.wait_ge(sem("ext_out"), 16)
            for t, dst in ((0, bias0), (1, bias1)):
                src = bass.AP(ext_dram.tensor, S - 1 - P * t, [[4 * 3 * P - 1, P], [3 * P, 4], [1, P * (t + 1)]])
                sp.dma_start(dst[:], src).then_inc(sem("bias_in"), 16)
            with sp.Fori(1, MOE_AT // RAW) as r:
                for i in range(RAW):
                    sp.wait_ge(sem("w_split"), r * RAW + (i + 1 - RAW))
                    sp.dma_start(raw[:, i, :], wst[bass.ds(r * RAW + i, 1)].rearrange("a p c -> p (a c)"))\
                      .then_inc(sem(f"raw_in{i}"), 16)
            for n in range(MOE_AT // RAW * RAW, MOE_AT + 2):
                sp.wait_ge(sem("w_split"), n + 1 - RAW)
                sp.dma_start(raw[:, n % RAW, :], wst[n]).then_inc(sem(f"raw_in{n % RAW}"), 16)

            def stream(first, source):
                with sp.Fori(0, NE * F_UNITS // RAW) as r:
                    for i in range(RAW):
                        sp.wait_ge(sem("w_split"), r * RAW + (first + i + 1 - RAW))
                        sp.dma_start(raw[:, (first + i) % RAW, :],
                                     wst[bass.ds(r * RAW + (source + i), 1)].rearrange("a p c -> p (a c)"))\
                          .then_inc(sem(f"raw_in{(first + i) % RAW}"), 16)

            stream(MOE_AT + 2, MOE_AT + 2)
            sp.wait_ge(sem("h_done"), 4)
            with sp.If(sp.value_load(over[0:1, 0:1], min_val=0, max_val=S) > P):
                for n in range(2):
                    sp.wait_ge(sem("w_split"), AGAIN_AT + n + 1 - RAW)
                    sp.dma_start(raw[:, (AGAIN_AT + n) % RAW, :], wst[MOE_AT + n])\
                      .then_inc(sem(f"raw_in{(AGAIN_AT + n) % RAW}"), 16)
                stream(AGAIN_AT + 2, MOE_AT + 2)
                sp.wait_ge(sem("h_done"), 5)
            sp.dma_start(out.rearrange("(t p) d -> p t d", p=P), h[:]).then_inc(sem("stored"), 16)
            sp.wait_ge(sem("stored"), 16)

        @block.scalar
        def _(e):
            act = e.activation

            def norm(n, split=True):
                e.wait_ge(sem("h_done"), n) if n else e.wait_ge(sem("x_in"), 16)
                for t in range(T):
                    act(xs[:, t, :], h[:, t, :], ACT.Square, accum_out=ssq[:, t:t + 1]).then_inc(sem("ssq"), 1)
                e.wait_ge(sem("ssq"), T * (n + 1))
                if n == 0:
                    e.wait_ge(sem("con_in"), 80)
                act(rstd, ssq, ACT.Sqrt, scale=1.0 / D, bias=C("eps", 0, 1)).then_inc(sem("rms"), 1)
                for j in range(4 if split else 0):
                    e.wait_ge(sem("xnf"), 4 * n + j + 1)
                    act(xhi[:, 2 * j:2 * j + 2, :], xnf[:, 2 * j:2 * j + 2, :], ACT.Copy).then_inc(sem("xhi"), 1)

            def z_evac(L, u):
                e.wait_ge(sem("w_used"), unit(L, u) + 1)
                dst, rows = z_at(u)
                src = bank[u % 2][:, 0:S]
                act(dst, src.rearrange("p (t c) -> p t c", t=T) if rows else src, ACT.Copy)\
                    .then_inc(sem("z_out"), 1)

            def zs_upto(L, a, b):
                for u in range(a, b):
                    z_evac(L, u)
                    hi(e, unit(L, u + RING))

            def y_high(L, j, name, n):
                e.wait_ge(sem(name), n)
                if j == 0:
                    e.wait_ge(sem("w_used"), unit(L, Z_UNITS))
                k = 2 * [2, 3, 0, 1][j]
                act(xhi[:, k:k + 2, :], yT[:, k:k + 2, :], ACT.Copy).then_inc(sem("yhi"), 1)

            def mixers(L):
                for u in range(RING):
                    hi(e, unit(L, u))
                norm(2 * L)
                zs_upto(L, 0, 7)
                e.wait_ge(sem("C_shift"), L + 1)
                act(lin[0:32, :], zs[0:32, 6, :], ACT.Tanh).then_inc(sem("C_lin"), 1)
                act(lin[32:64, :], zs[32:64, 6, :], ACT.Copy).then_inc(sem("C_lin"), 1)
                act(lin[64:128, :], zs[64:128, 6, :], ACT.Sigmoid).then_inc(sem("C_lin"), 1)
                e.wait_ge(sem("C_lora"), L + 1)
                for i in range(PAIRS):
                    act(sga[:, i, :], bank[3][:, i * S:(i + 1) * S], ACT.Sigmoid, bias=V(L, "a0", i))\
                        .then_inc(sem("C_sga"), 1)
                for i in range(PAIRS):
                    act(sgw[:, i, :], bank[2][:, i * S:(i + 1) * S], ACT.Sigmoid, bias=V(L, "w0", i))\
                        .then_inc(sem("C_sgw"), 1)
                act(gC, bank[4][:, :].rearrange("p (i s) -> p i s", i=PAIRS), ACT.Copy).then_inc(sem("C_g"), 1)
                zs_upto(L, 7, 8)
                e.wait_ge(sem("C_kk"), L + 1)
                act(sq, bank[5][:, :].rearrange("p (i s) -> p i s", i=2), ACT.Sqrt, scale=float(HD))\
                    .then_inc(sem("C_kn"), 1)
                zs_upto(L, 8, 9)
                e.wait_ge(sem("C_cum"), L + 1)
                act(cinv, cum, ACT.Exp, scale=KAPPA).then_inc(sem("C_exp"), 1)
                act(sgw, sgw, ACT.Exp, scale=-KAPPA).then_inc(sem("C_exp"), 1)
                act(alr[:, 1], cum, ACT.Exp, scale=-KAPPA).then_inc(sem("C_exp"), 1)
                zs_upto(L, 9, 11)
                for n, dst in enumerate((vtok, khtok, altok, betok)):
                    e.wait_ge(sem("C_tr"), 4 * L + n + 1)
                    act(dst, bank[2 + n][:, :].rearrange("p (t c) -> p t c", t=T), ACT.Copy)\
                        .then_inc(sem("C_tok"), 1)
                zs_upto(L, 11, 14)
                e.wait_ge(sem("C_bv"), L + 1)
                act(BVs, bank[2][:, :].rearrange("p (t i m v) -> p t i m v", t=T, i=PAIRS, m=2), ACT.Copy)\
                    .then_inc(sem("C_bvs"), 1)
                zs_upto(L, 14, 20)
                e.wait_ge(sem("C_w"), L + 1)
                act(Ws, bank[3][:, :].rearrange("p (t i v) -> p t i v", t=T, i=PAIRS), ACT.Copy)\
                    .then_inc(sem("C_ws"), 1)
                e.wait_ge(sem("C_xa"), L + 1)
                act(XA, bank[4][:, :].rearrange("p (a c) -> p a c", a=4), ACT.Copy).then_inc(sem("C_xas"), 1)
                zs_upto(L, 20, 24)
                e.wait_ge(sem("C_var"), L + 1)
                act(yc2, bank[6][:, :].rearrange("p (i s) -> p i s", i=2), ACT.Sqrt, bias=C("eps", 1, 2))\
                    .then_inc(sem("C_sd"), 1)
                y_high(L, 0, "y_C", L + 1)
                e.wait_ge(sem("D_abs"), L + 1)
                act(els, els, ACT.Exp).then_inc(sem("D_e"), 1)
                e.wait_ge(sem("D_e"), L + 1)
                act(els, els, ACT.Ln, bias=1.0).then_inc(sem("D_ln"), 1)
                e.wait_ge(sem("D_cum"), L + 1)
                act(eb, cumd, ACT.Exp, scale=1.0 / 16).then_inc(sem("D_exp"), 1)
                act(enb, cumd, ACT.Exp, scale=-1.0 / 16).then_inc(sem("D_exp"), 1)
                act(dl, dl, ACT.Exp, scale=1.0 / 16).then_inc(sem("D_exp"), 1)
                act(sgo, ogD, ACT.Silu).then_inc(sem("D_silu"), 1)
                e.wait_ge(sem("D_ktr"), L + 1)
                act(kltok, bank[4][:, 0:S].rearrange("p (t c) -> p t c", t=T), ACT.Copy).then_inc(sem("D_ktok"), 1)
                e.wait_ge(sem("D_ms"), L + 1)
                act(rsD, bank[4][:, :].rearrange("p (i s) -> p i s", i=2), ACT.Sqrt, bias=C("eps", 0, 1))\
                    .then_inc(sem("D_rms"), 1)
                for n in range(2):
                    e.wait_ge(sem("A_ms"), 2 * L + n + 1)
                    act(sqA[:, 2 * n:2 * n + 2, :], bank[5 + n][:, :].rearrange("p (i s) -> p i s", i=2), ACT.Sqrt,
                        bias=C("eps", 0, 1)).then_inc(sem("A_rms"), 1)
                y_high(L, 1, "y_D", L + 1)
                for t in range(T):
                    e.wait_ge(sem("A_max"), T * L + t + 1)
                    for hh in range(4):
                        s = (s0 if t == 0 else s1)[:, hh, :]
                        act(s, s, ACT.Exp, bias=negm[:, 4 * t + hh:4 * t + hh + 1],
                            accum_out=den[:, 4 * t + hh:4 * t + hh + 1]).then_inc(sem("A_exp"), 1)
                for n, b in enumerate((5, 6, 2)):
                    e.wait_ge(sem("A_tr"), 3 * L + n + 1)
                    act(pt[:, 4 * n:4 * n + 4, :], bank[b][:, :].rearrange("p (a c) -> p a c", a=4), ACT.Copy)\
                        .then_inc(sem("A_pt"), 1)
                for i in range(PAIRS):
                    e.wait_ge(sem("A_pv"), 2 * L + i + 1)
                    act(yT[:, i, :], bank[3 + i][:, 0:S], ACT.Copy).then_inc(sem("y_A"), 1)
                y_high(L, 2, "y_A", 2 * L + 2)
                e.wait_ge(sem("B_go"), L + 1)
                act(sgb, gB, ACT.Sigmoid).then_inc(sem("B_sig"), 1)
                e.wait_ge(sem("B_var"), L + 1)
                act(sqB, bank[4][:, :].rearrange("p (i s) -> p i s", i=2), ACT.Sqrt, bias=C("eps", 2, 3))\
                    .then_inc(sem("B_sd"), 1)
                e.wait_ge(sem("B_ln"), L + 1)
                act(yT[:, 2:4, :], acc, ACT.Silu).then_inc(sem("y_B"), 1)
                y_high(L, 3, "y_B", L + 1)
                hi(e, unit(L, 30))
                hi(e, unit(L, 31))

            e.wait_ge(sem("ext_mm"), 1)
            for hh, b in enumerate((0, 1, 6, 7)):
                act(ext[:, hh, :], bank[b][:, 0:3 * P], ACT.Copy).then_inc(sem("ext_sb"), 1)

            def silu(j, first=None, reg=None):
                wait_gate_up(e, j, first, reg)
                if j >= 2:
                    e.wait_ge(sem("hm"), at(reg, FB, j - 1))
                act(sg[:, j % 2, :], bank[j % 2][:, 0:P], ACT.Silu).then_inc(sem("silu"), 1)

            def hidden_high(j, first=None, reg=None):
                e.wait_ge(sem("ht"), at(reg, FB, j + 1))
                if j >= 2:
                    wait_down(e, j, first, reg, before=2)
                act(hthi[:, j % 2, :], bank[2][:, 0:P], ACT.Copy).then_inc(sem("hthi"), 1)

            def dense():
                hi(e, DENSE_AT)
                hi(e, DENSE_AT + 1)
                norm(1)
                for b in range(FB):
                    hi(e, DENSE_AT + 3 * b + 2)
                    if b > 0:
                        hidden_high(2 * b - 1)
                    silu(2 * b)
                    if b < FB - 1:
                        hi(e, DENSE_AT + 3 * b + 3)
                    hidden_high(2 * b)
                    if b < FB - 1:
                        hi(e, DENSE_AT + 3 * b + 4)
                    silu(2 * b + 1)
                hidden_high(2 * FB - 1)

            def x_high(reg, v):
                for k in range(2):
                    e.wait_ge(sem("M_xgf"), at(reg, 2, 2 * v + k + 1))
                    act(xhi[:, 4 * k:4 * k + 4, 0:P], xgf[:, 4 * k:4 * k + 4, :], ACT.Copy)\
                        .then_inc(sem("M_xhi"), 1)

            def experts(again, first, j0):
                hi(e, first)
                hi(e, first + 1)
                v0 = (NE + 1) * again
                x_high(None, v0)
                with e.Fori(0, NE) as ex:
                    for b in range(FB):
                        j, u = j0 + b, first + 2 + 3 * b
                        hi(e, u, ex)
                        if b > 0:
                            hidden_high(j - 1, first, ex)
                        hi(e, u + 1, ex)
                        hi(e, u + 2, ex)
                        silu(j, first, ex)
                        if b == 5:
                            e.wait_ge(sem("M_selgt"), ex + (NE * again + 1))
                            act(selgt, bank[5][:, 0:S].rearrange("p (t c) -> p t c", t=T), ACT.Copy)\
                                .then_inc(sem("M_selgts"), 1)
                    hidden_high(j0 + FB - 1, first, ex)
                    x_high(ex, v0 + 1)
                    wait_down(e, j0 + FB - 1, first, ex)
                    for n in range(2):
                        act(ysb[:, 512 * n:512 * n + 512], bank[3 + n][:, :], ACT.Copy).then_inc(sem("M_y"), 1)

            if stop >= 1:
                mixers(0)
            if stop >= 2:
                dense()
            if stop >= 3:
                mixers(1)
            if stop >= 4:
                norm(3, split=False)
                e.wait_ge(sem("R_dif"), 1)
                act(dif, dif, ACT.Exp).then_inc(sem("R_exp"), 1)
                experts(0, MOE_AT, 2 * FB)
                e.wait_ge(sem("R_over"), 1)
                with e.If(e.value_load(over[0:1, 0:1], min_val=0, max_val=S) > P):
                    experts(1, AGAIN_AT, 2 * FB + NE * FB)

        @block.tensor
        def _(e):
            mm = e.matmul

            def norm(n):
                for j in range(4):
                    for kk in range(2):
                        for t in range(T):
                            if j == 0 and kk == 0:
                                e.wait_ge(sem("xs"), T * n + t + 1)
                            k = 2 * j + kk
                            c = (2 * kk + t) * P
                            ins = e.transpose(bank[2 + j][:, c:c + P], xs[:, t, k * P:(k + 1) * P], ident)
                    ins.then_inc(sem("xn_t"), 1)

            def three(out_, w, x_, start, stop_, w_left):
                (wh, wl), (xh, xl) = w, x_
                for n, (a, b) in enumerate(((wh, xh), (wh, xl), (wl, xh)) if w_left
                                           else ((xh, wh), (xh, wl), (xl, wh))):
                    ins = mm(out_, a, b, start=start and n == 0, stop=stop_ and n == 2, skip_group_check=True)
                return ins

            def zs_upto(L, a, b):
                for u in range(a, b):
                    n = unit(L, u)
                    if u == 0:
                        e.wait_ge(sem("x_split"), 4 * (2 * L + 1))
                    e.wait_ge(sem("w_split"), n + 1)
                    if u >= 2:
                        e.wait_ge(sem("z_out"), Z_UNITS * L + u - 1)
                    s, (_, rows) = n % RING, z_at(u)
                    for t in range(T if rows else 1):
                        for k in range(KD):
                            w = [a_[:, s, k * P:(k + 1) * P] for a_ in (whi, wlo)]
                            c = slice(t * P, (t + 1) * P) if rows else slice(0, S)
                            ins = three(bank[u % 2][:, c], w, [a_[:, k, c] for a_ in (xhi, xlo)],
                                        k == 0, k == KD - 1, not rows)
                    ins.then_inc(sem("w_used"), 1)

            def project(L, j):
                e.wait_ge(sem("y_split"), 4 * L + j + 1)
                for i in range(2):
                    n = unit(L, Z_UNITS + 2 * j + i)
                    e.wait_ge(sem("w_split"), n + 1)
                    s, k = n % RING, 2 * [2, 3, 0, 1][j] + i
                    for t in range(T):
                        for half in range(2):
                            b = PROJ[2 * t + half]
                            w = [a_[:, s, half * 512:half * 512 + 512] for a_ in (whi, wlo)]
                            ins = three(bank[b][:, :], w, [a_[:, k, t * P:(t + 1) * P] for a_ in (xhi, xlo)],
                                        j == 0 and i == 0, j == 3 and i == 1, False)
                    ins.then_inc(sem("w_used"), 1)

            def mixers(L):
                norm(2 * L)
                zs_upto(L, 0, 8)
                e.wait_ge(sem("C_lin"), 3 * (L + 1))
                for q in range(3):
                    for i in range(PAIRS):
                        ins = mm(bank[2 + q][:, i * S:(i + 1) * S], lor[:, L, q, i * P:(i + 1) * P], lin,
                                 start=True, stop=True)
                ins.then_inc(sem("C_lora"), 1)
                zs_upto(L, 8, 9)
                e.wait_ge(sem("C_sq"), L + 1)
                mm(bank[5][:, :], blk, sq, start=True, stop=True).then_inc(sem("C_kk"), 1)
                zs_upto(L, 9, 10)
                e.wait_ge(sem("C_rk"), L + 1)
                mm(bank[6][:, :], blk, bonus, start=True, stop=True).then_inc(sem("C_bon"), 1)
                zs_upto(L, 10, 11)
                e.wait_ge(sem("C_g"), L + 1)
                for n, (src, ready) in enumerate(((zs[:, 4:6, :], 0), (knew, 1), (alr[:, 0], 2), (kkn, 3))):
                    e.wait_ge(sem("C_shift"), L + 1) if n == 0 else e.wait_ge(sem("C_in"), 3 * L + n)
                    for t in range(T):
                        for i in range(PAIRS):
                            ins = e.transpose(bank[2 + n][:, (2 * t + i) * P:(2 * t + i + 1) * P],
                                              src[:, i, t * P:(t + 1) * P], ident)
                    ins.then_inc(sem("C_tr"), 1)
                zs_upto(L, 11, 12)
                e.wait_ge(sem("C_rh"), L + 1)
                order = (6, 7, 2, 3, 4, 5)
                for n in range(8):
                    i, t, m = n // 4, n // 2 % 2, n % 2
                    if n == 2:
                        e.wait_ge(sem("C_tok"), 4 * (L + 1))
                    if n >= 6:
                        e.wait_ge(sem("C_mats"), 8 * L + n - 5)
                    hp, tok = slice(m * HD, (m + 1) * HD), slice(t * P, (t + 1) * P)
                    for q, src in enumerate((kkn, knew)):
                        ins = mm(bank[order[n % 6]][:, q * S:(q + 1) * S], src[hp, i, tok], alr[hp, :, i, tok],
                                 start=True, stop=True)
                    ins.then_inc(sem("C_mat"), 1)
                zs_upto(L, 12, 14)
                e.wait_ge(sem("C_mats"), 8 * (L + 1))
                for n in range(8):
                    i, t, m = n // 4, n // 2 % 2, n % 2
                    c = ((t * PAIRS + i) * 2 + m) * HD
                    ins = mm(bank[2][:, c:c + HD], mats[:, n, 2, :], vtok[:, t, i * P + m * HD:i * P + m * HD + HD],
                             start=True, stop=True)
                ins.then_inc(sem("C_bv"), 1)
                e.wait_ge(sem("C_x0"), L + 1)
                for l in range(LEVELS):
                    k = LEVELS * L + l
                    for g in range(2):
                        if l > 0:
                            e.wait_ge(sem("C_x"), 2 * (k - 1) + g + 1)
                        for n in range(4 * g, 4 * g + 4):
                            ins = mm(bank[3 + g][:, (n % 4) * P:(n % 4 + 1) * P], mats[:, n, 0, :], X[:, n, :],
                                     start=True, stop=True)
                        ins.then_inc(sem("C_m1"), 1)
                    for g in range(2):
                        e.wait_ge(sem("C_m1s"), 2 * k + g + 1)
                        if g == 1 and l == 0:
                            e.wait_ge(sem("C_bvs"), L + 1)
                        if l < LEVELS - 1:
                            for n in range(4 * g, 4 * g + 4):
                                mm(bank[5 + g][:, (n % 4) * P:(n % 4 + 1) * P], XT[:, n, :], mats[:, n, 2, :],
                                   start=True, stop=True)
                        for n in range(4 * g, 4 * g + 4):
                            ins = mm(bank[(7, 2)[g]][:, (n % 4) * P:(n % 4 + 1) * P], mats[:, n, 2, :], XT[:, n, :],
                                     start=True, stop=True)
                        ins.then_inc(sem("C_p"), 1)
                    zs_upto(L, 14 + l, 15 + l)
                e.wait_ge(sem("C_x"), 2 * LEVELS * (L + 1))
                for n in range(8):
                    i, t, m = n // 4, n // 2 % 2, n % 2
                    c = ((t * PAIRS + i) * 2 + m) * HD
                    ins = mm(bank[3][:, c:c + HD], XT[:, n, :], BVs[:, t, i, m, :], start=True, stop=True)
                ins.then_inc(sem("C_w"), 1)
                for n in range(8):
                    i, t, m = n // 4, n // 2 % 2, n % 2
                    ins = mm(bank[4][m * HD:(m + 1) * HD, (2 * i + t) * P:(2 * i + t + 1) * P],
                             altok[:, t, i * P + m * HD:i * P + m * HD + HD], XT[:, n, :], start=True, stop=True,
                             skip_group_check=True)
                ins.then_inc(sem("C_xa"), 1)
                e.wait_ge(sem("C_xas"), L + 1)
                for c in range(NCH):
                    t, hf = c // 2, c % 2
                    rows = slice(hf * HD, (hf + 1) * HD)
                    e.wait_ge(sem("C_st"), NCH * L + c + 1)
                    for i in range(PAIRS):
                        ins = mm(bank[5][rows, i * P:(i + 1) * P], XA[:, 2 * i + t, rows], ST[:, c, i, :],
                                 start=True, stop=True, skip_group_check=True)
                    ins.then_inc(sem("C_u"), 1)
                    if c < NCH - 1:
                        e.wait_ge(sem("C_us"), NCH * L + c + 1)
                        for i in range(PAIRS):
                            cols = slice(i * P, (i + 1) * P)
                            mm(bank[6][:, cols], betok[rows, t, cols], Us[rows, t, i, :], start=True, stop=False,
                               skip_group_check=True)
                            ins = mm(bank[6][:, cols], khtok[rows, t, cols], vtok[rows, t, cols], start=False,
                                     stop=True, skip_group_check=True)
                        ins.then_inc(sem("C_ds"), 1)
                    zs_upto(L, 20 + c, 21 + c)
                e.wait_ge(sem("C_us"), NCH * (L + 1))
                e.wait_ge(sem("C_ws"), L + 1)
                for i in range(PAIRS):
                    for c in range(NCH):
                        tok = slice(c * CHUNK, (c + 1) * CHUNK)
                        mm(bank[3 + i][:, tok], ST[:, c, i, :], alr[:, 1, i, tok], start=c == 0, stop=False,
                           skip_group_check=True)
                    for t in range(T):
                        for m in range(2):
                            n = 4 * i + 2 * t + m
                            o = bank[3 + i][m * HD:(m + 1) * HD, t * P:(t + 1) * P]
                            mm(o, Us[:, t, i, m * HD:(m + 1) * HD], mats[:, n, 1, :], start=False, stop=False,
                               skip_group_check=True)
                            ins = mm(o, vtok[:, t, i * P + m * HD:i * P + (m + 1) * HD], mats[:, n, 3, :],
                                     start=False, stop=True, skip_group_check=True)
                    ins.then_inc(sem("C_o"), 1)
                e.wait_ge(sem("C_oc"), L + 1)
                mm(bank[5][:, :], blk, yC, start=True, stop=True).then_inc(sem("C_mean"), 1)
                e.wait_ge(sem("C_xc"), L + 1)
                mm(bank[6][:, :], blk, yc2, start=True, stop=True).then_inc(sem("C_var"), 1)
                mm(bank[7][:, 0:S], g2s[:, L, :], gdD[0:16, :], start=True, stop=True).then_inc(sem("D_gk"), 1)
                e.wait_ge(sem("D_qx"), L + 1)
                for t in range(T):
                    ins = mm(bank[2 + t][:, :], kd[:, t * P:(t + 1) * P], qx[:, :, t * P:(t + 1) * P],
                             start=True, stop=True)
                    ins.then_inc(sem("D_att"), 1)
                for t in range(T):
                    ins = e.transpose(bank[4][:, t * P:(t + 1) * P], kl[:, t * P:(t + 1) * P], ident)
                ins.then_inc(sem("D_ktr"), 1)
                e.wait_ge(sem("D_ktok"), L + 1)
                for c in range(NCH - 1):
                    rows = slice((c % 2) * HD, (c % 2 + 1) * HD)
                    ins = mm(bank[5 + c][:, 0:GROUP], kltok[rows, c // 2, :], vD[rows, c // 2, :],
                             start=True, stop=True)
                    ins.then_inc(sem("D_con"), 1)
                e.wait_ge(sem("D_atts"), T * (L + 1))
                for i in range(PAIRS):
                    for t in range(T):
                        for m in range(2):
                            hh = 2 * i + m
                            mm(bank[2 + i][m * HD:(m + 1) * HD, t * P:(t + 1) * P], vD[:, t, hh * HD:(hh + 1) * HD],
                               attD[:, t, hh, :], start=t == 0, stop=False, skip_group_check=True)
                    for c in range(1, NCH):
                        e.wait_ge(sem("D_st"), (NCH - 1) * L + c)
                        tok = slice(c * CHUNK, (c + 1) * CHUNK)
                        ins = mm(bank[2 + i][:, tok], SD[:, c, i * P:(i + 1) * P], qd[:, tok], start=False,
                                 stop=c == NCH - 1, skip_group_check=True)
                    ins.then_inc(sem("D_o"), 1)
                e.wait_ge(sem("D_sq"), L + 1)
                mm(bank[4][:, :], blk, sqD, start=True, stop=True).then_inc(sem("D_ms"), 1)
                for n in range(2):
                    e.wait_ge(sem("A_sq"), 2 * L + n + 1)
                    mm(bank[5 + n][:, :], blk, sqA[:, 2 * n:2 * n + 2, :], start=True, stop=True)\
                        .then_inc(sem("A_ms"), 1)
                e.wait_ge(sem("A_qk"), L + 1)
                for n, b in enumerate((2, 3, 4, 7)):
                    t, i = n // 2, n % 2
                    kj = P * (t + 1)
                    mm(bank[b][:, 0:2 * kj], qn[:, i, t * P:(t + 1) * P], kx[:, :, i, 0:kj], start=True, stop=True)\
                        .then_inc(sem("A_s"), 1)
                for n, b in enumerate((5, 6, 2)):
                    e.wait_ge(sem("A_p"), T * L + (1 if n == 0 else 2))
                    for q in range(4):
                        if n == 0:
                            src = s0[:, q, :]
                        else:
                            src = s1[:, 2 * (n - 1) + q // 2, (q % 2) * P:(q % 2 + 1) * P]
                        ins = e.transpose(bank[b][:, q * P:(q + 1) * P], src, ident)
                    ins.then_inc(sem("A_tr"), 1)
                e.wait_ge(sem("A_pt"), 3 * (L + 1))
                for i in range(PAIRS):
                    for m in range(2):
                        hh = 2 * i + m
                        o = bank[3 + i][m * HD:(m + 1) * HD, :]
                        vv = [vA[:, jt, hh * HD:(hh + 1) * HD] for jt in range(T)]
                        mm(o[:, 0:P], vv[0], pt[:, hh, :], start=True, stop=False, skip_group_check=True)
                        mm(o[:, P:S], vv[0], pt[:, 4 + 2 * hh, :], start=False, stop=False, skip_group_check=True)
                        ins = mm(o[:, P:S], vv[1], pt[:, 5 + 2 * hh, :], start=False, stop=True,
                                 skip_group_check=True)
                    ins.then_inc(sem("A_pv"), 1)
                e.wait_ge(sem("B_acc"), L + 1)
                mm(bank[3][:, :], blk, acc, start=True, stop=True).then_inc(sem("B_mean"), 1)
                e.wait_ge(sem("B_xc"), L + 1)
                mm(bank[4][:, :], blk, sqB, start=True, stop=True).then_inc(sem("B_var"), 1)
                for j in range(4):
                    project(L, j)

            e.wait_ge(sem("ext_in"), 32)
            for hh, b in enumerate((0, 1, 6, 7)):
                ins = mm(bank[b][:, 0:3 * P], rel[:, hh, :], bkt[0:32, :], start=True, stop=True)
            ins.then_inc(sem("ext_mm"), 1)
            e.wait_ge(sem("con_in"), 80)

            def gate_up(j, part, unit_, tok, reg=None):
                e.wait_ge(sem("w_split"), at(reg, F_UNITS, unit_ + 1))
                if part == 0 and j >= 2:
                    e.wait_ge(sem("hm"), at(reg, FB, j - 1))
                s = unit_ % RING
                for k in range(4):
                    w = [a_[:, s, k * 256:(k + 1) * 256] for a_ in (whi, wlo)]
                    ins = three(bank[j % 2][:, 0:256], w, [a_[:, 4 * part + k, tok] for a_ in (xhi, xlo)],
                                part == 0 and k == 0, part == 1 and k == 3, False)
                return ins

            def turn(j, reg=None):
                e.wait_ge(sem("hm"), at(reg, FB, j + 1))
                e.transpose(bank[2][:, 0:P], hm[:, j % 2, :], ident).then_inc(sem("ht"), 1)

            def down(j, unit_, banks, start, stop_, reg=None):
                e.wait_ge(sem("htlo"), at(reg, FB, j + 1))
                e.wait_ge(sem("w_split"), at(reg, F_UNITS, unit_ + 1))
                s = unit_ % RING
                for half in range(2):
                    w = [a_[:, s, half * 512:half * 512 + 512] for a_ in (whi, wlo)]
                    ins = three(bank[banks[half]][:, :], w, [a_[:, j % 2, :] for a_ in (hthi, htlo)],
                                start, stop_, False)
                return ins

            def dense():
                norm(1)
                e.wait_ge(sem("x_split"), 8)
                for j in range(2 * FB + 1):
                    b, t = j // 2, j % 2
                    n = DENSE_AT + 3 * b
                    tok = slice(t * P, (t + 1) * P)
                    pb_, pt_ = (j - 1) // 2, (j - 1) % 2
                    if j < 2 * FB:
                        ins = gate_up(j, 0, n, tok)
                        if t == 1:
                            ins.then_inc(sem("w_used"), 1)
                    if j > 0:
                        turn(j - 1)
                    if j < 2 * FB:
                        gate_up(j, 1, n + 1, tok).then_inc(sem("w_used" if t == 1 else "gu"), 1)
                    if j > 0:
                        ins = down(j - 1, DENSE_AT + 3 * pb_ + 2, (3 + 2 * pt_, 4 + 2 * pt_), pb_ == 0,
                                   pb_ == FB - 1)
                        ins.then_inc(sem("w_used" if pt_ == 1 else "down"), 1)

            def gather_half(k2, reg, v):
                e.wait_ge(sem("M_sel"), at(reg, 1, v + 1))
                if k2 == 1:
                    e.wait_ge(sem("M_xgf"), at(reg, 2, 2 * v + 1))
                for k in range(4):
                    for t in range(T):
                        kk = 4 * k2 + k
                        ins = mm(bank[5][:, k * P:(k + 1) * P], xs[:, t, kk * P:(kk + 1) * P], sel[:, t, :],
                                 start=t == 0, stop=t == 1, skip_group_check=True)
                ins.then_inc(sem("M_gath"), 1)

            def experts(again, first, j0):
                v0 = (NE + 1) * again
                gather_half(0, None, v0)
                gather_half(1, None, v0)
                tok = slice(0, P)
                with e.Fori(0, NE) as ex:
                    for k in range(2):
                        e.wait_ge(sem("M_xlo"), ex * 2 + (2 * v0 + k + 1))
                    for b in range(FB + 1):
                        j = j0 + b
                        if b < FB:
                            u = first + gu_unit(b)
                            gate_up(j, 0, u, tok, ex).then_inc(sem("w_used"), 1)
                        if b > 0:
                            turn(j - 1, ex)
                        if b < FB:
                            gate_up(j, 1, u + 1, tok, ex).then_inc(sem("w_used"), 1)
                        if b > 0:
                            down(j - 1, first + wd_unit(b - 1), (3, 4), b == 1, b == FB, ex)\
                                .then_inc(sem("w_used"), 1)
                        if b == 4:
                            e.wait_ge(sem("M_selg"), ex + (NE * again + 1))
                            for t in range(T):
                                ins = e.transpose(bank[5][:, t * P:(t + 1) * P], selg[:, t, :], ident)
                            ins.then_inc(sem("M_selgt"), 1)
                        if b == 8:
                            e.wait_ge(sem("M_selgts"), ex + (NE * again + 1))
                            gather_half(0, ex, v0 + 1)
                        if b == 12:
                            gather_half(1, ex, v0 + 1)
                    for n in range(4):
                        t, half = n // 2, n % 2
                        if n < 2:
                            e.wait_ge(sem("M_y"), ex * 2 + (2 * NE * again + n + 1))
                        else:
                            e.wait_ge(sem("M_add"), ex * 4 + (4 * NE * again + n - 1))
                        mm(bank[6 + half][:, :], selgt[:, t, :], ysb[:, 512 * half:512 * half + 512],
                           start=True, stop=True).then_inc(sem("M_comb"), 1)

            if stop >= 1:
                mixers(0)
            if stop >= 2:
                dense()
            if stop >= 3:
                mixers(1)
            if stop >= 4:
                norm(3)
                e.wait_ge(sem("xnf"), 16)
                for t in range(T):
                    for k in range(KD):
                        ins = mm(bank[6 + t][:, 0:NE], xnf[:, k, t * P:(t + 1) * P], rou[:, k, :],
                                 start=k == 0, stop=k == KD - 1)
                    ins.then_inc(sem("R_lg"), 1)
                e.wait_ge(sem("R_mk"), 1)
                mm(bank[2][:, 0:8], C("upper"), mk[:, 0, :], start=True, stop=True)
                mm(bank[2][:, 8:16], C("upper"), mk[:, 1, :], start=True, stop=False)
                mm(bank[2][:, 8:16], C("ones"), mk[:, 0, :], start=False, stop=True)
                mm(bank[2][:, 16:24], C("ones"), mk[:, 0, :], start=True, stop=False)
                mm(bank[2][:, 16:24], C("ones"), mk[:, 1, :], start=False, stop=True).then_inc(sem("R_rank"), 1)
                experts(0, MOE_AT, 2 * FB)
                e.wait_ge(sem("R_over"), 1)
                with e.If(e.value_load(over[0:1, 0:1], min_val=0, max_val=S) > P):
                    experts(1, AGAIN_AT, 2 * FB + NE * FB)

        @block.vector
        def _(e):
            ch = Chain(e, sem("dve_chain"))
            tt, ts, stt = e.tensor_tensor, e.tensor_scalar, e.scalar_tensor_tensor

            def norm(n, split=True):
                e.wait_ge(sem("rms"), n + 1)
                ch(e.reciprocal(rstd, rstd))
                for t in range(T):
                    ts(xs[:, t, :], h[:, t, :], rstd[:, t:t + 1], None, ALU.mult).then_inc(sem("xs"), 1)
                g = V(n // 2, "mix_g" if n % 2 == 0 else "ffn_g", 0, KD)
                for j in range(4):
                    e.wait_ge(sem("xn_t"), 4 * n + j + 1)
                    tt(xnf[:, 2 * j:2 * j + 2, :], bank[2 + j][:, :].rearrange("p (k s) -> p k s", k=2),
                       g[:, 2 * j:2 * j + 2].unsqueeze(2).to_broadcast([P, 2, S]), ALU.mult)\
                        .then_inc(sem("xnf"), 1)
                    if split:
                        e.wait_ge(sem("xnf"), 4 * n + j + 1)
                        e.wait_ge(sem("xhi"), 4 * n + j + 1)
                        tt(xlo[:, 2 * j:2 * j + 2, :], xnf[:, 2 * j:2 * j + 2, :],
                           xhi[:, 2 * j:2 * j + 2, :].bitcast(F32), ALU.subtract).then_inc(sem("x_split"), 1)

            def los(L, a, b):
                for u in range(a, b):
                    lo(e, unit(L, u))

            def y_low(L, j, name, n):
                e.wait_ge(sem("yhi"), 4 * L + j + 1)
                e.wait_ge(sem(name), n)
                k = 2 * [2, 3, 0, 1][j]
                tt(xlo[:, k:k + 2, :], yT[:, k:k + 2, :], xhi[:, k:k + 2, :].bitcast(F32), ALU.subtract)\
                    .then_inc(sem("y_split"), 1)

            def mixers(L):
                los(L, 0, RING)
                norm(2 * L)
                e.memset(zC[:, :, 0:1], 0.0).then_inc(sem("C_zero"), 1)
                e.memset(hB[:, :, 0:CW - 1], 0.0).then_inc(sem("B_zero"), 1)
                los(L, RING, RING + 6)
                if L == 0:
                    e.wait_ge(sem("bias_in"), 32)
                    lm = C("logm")
                    ch(tt(bias0[:], bias0[:], over4(lm[:, 0:P]), ALU.add))
                    ch(tt(bias1[:], bias1[:], lm[:, P:3 * P].unsqueeze(1).to_broadcast([P, 4, S]), ALU.add))
                e.wait_ge(sem("z_out"), Z_UNITS * L + 7)
                e.wait_ge(sem("C_zero"), L + 1)
                ch(tt(zs, zC[:, :, 0:S], zC[:, :, 1:S + 1], ALU.subtract))
                for u in (6, 4, 5, 2, 3, 0, 1):
                    ins = stt(zs[:, u, :], zs[:, u, :], V(L, "mu", u), zC[:, u, 1:S + 1], ALU.mult, ALU.add)
                ins.then_inc(sem("C_shift"), 1)
                e.wait_ge(sem("C_shift"), L + 1)
                for i in range(PAIRS):
                    ins = ts(kkn[:, i, :], zs[:, 2 + i, :], V(L, "k_k", i), None, ALU.mult)
                ch(ins)
                tt(sq, kkn, kkn, ALU.mult).then_inc(sem("C_sq"), 1)
                for m in (X, XT):
                    for g in range(2):
                        ins = e.tensor_copy(m[:, 4 * g:4 * g + 4, :], over4(ident))
                ins.then_inc(sem("C_x0"), 1)
                e.wait_ge(sem("C_sga"), 2 * (L + 1))
                for i in range(PAIRS):
                    ins = ts(knew[:, i, :], sga[:, i, :], 1.0, V(L, "k_a", i), ALU.subtract, ALU.mult)
                ch(ins)
                ch(stt(knew, knew, 1.0, zs[:, 2:4, :], ALU.add, ALU.mult))
                for i in range(PAIRS):
                    ins = stt(bonus[:, i, :], zs[:, i, :], V(L, "r_k", i), knew[:, i, :], ALU.mult, ALU.mult)
                ins.then_inc(sem("C_rk"), 1)
                los(L, RING + 6, RING + 7)
                e.wait_ge(sem("C_sgw"), 2 * (L + 1))
                for i in range(PAIRS):
                    ins = e.tensor_tensor_scan(cum[:, i, :], C("restart"), sgw[:, i, :], 0.0, ALU.mult, ALU.add)
                ch(ins)
                tt(sgw, cum, sgw, ALU.subtract).then_inc(sem("C_cum"), 1)
                e.wait_ge(sem("C_kn"), L + 1)
                ch(ts(sq, sq, 1e-12, None, ALU.max))
                ch(e.reciprocal(sq, sq))
                ch(tt(kkn, sq, kkn, ALU.mult))
                ch(tt(sga, kkn, sga, ALU.mult))
                e.wait_ge(sem("C_bon"), L + 1)
                stt(bonus, bank[6][:, :].rearrange("p (i s) -> p i s", i=2), float(HD), zs[:, 4:6, :],
                    ALU.mult, ALU.mult).then_inc(sem("C_bonus"), 1)
                e.wait_ge(sem("C_exp"), 3 * L + 1)
                tt(knew, knew, cinv, ALU.mult).then_inc(sem("C_in"), 1)
                e.wait_ge(sem("C_exp"), 3 * L + 2)
                stt(alr[:, 0], kkn, -1.0, sgw, ALU.mult, ALU.mult).then_inc(sem("C_in"), 1)
                e.wait_ge(sem("C_in"), 3 * L + 2)
                tt(kkn, sga, cinv, ALU.mult).then_inc(sem("C_in"), 1)
                e.wait_ge(sem("C_exp"), 3 * L + 3)
                ch(e.tensor_copy(cend, alr[:, 1].rearrange("p i (c s) -> p i c s", s=CHUNK)[:, :, :, CHUNK - 1]))
                tt(alr[:, 1], alr[:, 1], zs[:, 0:2, :], ALU.mult).then_inc(sem("C_rh"), 1)
                los(L, RING + 7, RING + 8)
                e.wait_ge(sem("C_in"), 3 * (L + 1))
                e.memset(ST, 0.0).then_inc(sem("C_st"), 1)
                order = (6, 7, 2, 3, 4, 5)
                for n in range(8):
                    e.wait_ge(sem("C_mat"), 8 * L + n + 1)
                    tt(mats[:, n, :, :], bank[order[n % 6]][:, :].rearrange("p (a c) -> p a c", a=4),
                       C("mask_g").rearrange("p (a c) -> p a c", a=4), ALU.mult).then_inc(sem("C_mats"), 1)
                los(L, RING + 8, RING + 11)
                e.wait_ge(sem("C_bv"), L + 1)
                e.wait_ge(sem("C_x0"), L + 1)
                for l in range(LEVELS):
                    k = LEVELS * L + l
                    for g in range(2):
                        e.wait_ge(sem("C_m1"), 2 * k + g + 1)
                        tt(mats[:, 4 * g:4 * g + 4, 2, :], bank[3 + g][:, :].rearrange("p (a c) -> p a c", a=4),
                           over4(C("lvl", l * P, (l + 1) * P)), ALU.mult).then_inc(sem("C_m1s"), 1)
                    for g in range(2):
                        e.wait_ge(sem("C_p"), 2 * k + g + 1)
                        four = slice(4 * g, 4 * g + 4)
                        if l < LEVELS - 1:
                            tt(X[:, four, :], X[:, four, :], bank[5 + g][:, :].rearrange("p (a c) -> p a c", a=4),
                               ALU.add)
                        tt(XT[:, four, :], XT[:, four, :],
                           bank[(7, 2)[g]][:, :].rearrange("p (a c) -> p a c", a=4), ALU.add)\
                            .then_inc(sem("C_x"), 1)
                    los(L, RING + 11 + l, RING + 12 + l)
                e.wait_ge(sem("C_ws"), L + 1)
                for c in range(NCH):
                    t, rows = c // 2, slice((c % 2) * HD, (c % 2 + 1) * HD)
                    if c < NCH - 1:
                        e.wait_ge(sem("C_st"), NCH * L + c + 1)
                        for i in range(PAIRS):
                            ins = ts(stc[:, i, :], ST[:, c, i, :], cend[:, i, c:c + 1], None, ALU.mult)
                        ch(ins)
                    e.wait_ge(sem("C_u"), NCH * L + c + 1)
                    tt(Us[rows, t, :, :], bank[5][rows, 0:S].rearrange("p (i v) -> p i v", i=PAIRS),
                       Ws[rows, t, :, :], ALU.add).then_inc(sem("C_us"), 1)
                    if c < NCH - 1:
                        e.wait_ge(sem("C_ds"), (NCH - 1) * L + c + 1)
                        for i in range(PAIRS):
                            for m in range(2):
                                d = slice(m * HD, (m + 1) * HD)
                                ins = stt(ST[d, c + 1, i, d], bank[6][d, i * P + m * HD:i * P + (m + 1) * HD],
                                          cend[d, i, c:c + 1], stc[d, i, d], ALU.mult, ALU.add)
                        ins.then_inc(sem("C_st"), 1)
                    los(L, RING + 17 + c, RING + 18 + c)
                for i in range(PAIRS):
                    e.wait_ge(sem("C_o"), 2 * L + i + 1)
                    ins = e.tensor_copy(yC[:, i, :], bank[3 + i][:, 0:S])
                ins.then_inc(sem("C_oc"), 1)
                e.wait_ge(sem("C_oc"), L + 1)
                e.wait_ge(sem("C_mean"), L + 1)
                ch(tt(yC, yC, bank[5][:, :].rearrange("p (i s) -> p i s", i=2), ALU.subtract))
                tt(yc2, yC, yC, ALU.mult).then_inc(sem("C_xc"), 1)
                los(L, RING + 21, RING + 23)
                e.wait_ge(sem("C_sd"), L + 1)
                ch(e.reciprocal(yc2, yc2))
                ch(tt(yC, yC, yc2, ALU.mult))
                for i in range(PAIRS):
                    ins = ts(yC[:, i, :], yC[:, i, :], V(L, "ln_g", i), V(L, "ln_b", i), ALU.mult, ALU.add)
                ch(ins)
                ch(tt(yC, yC, bonus, ALU.add))
                tt(yT[:, 4:6, :], yC, gC, ALU.mult).then_inc(sem("y_C"), 1)
                y_low(L, 0, "y_C", L + 1)
                los(L, RING + 23, RING + 24)
                e.wait_ge(sem("z_out"), Z_UNITS * (L + 1))
                e.wait_ge(sem("D_gk"), L + 1)
                ch(ts(cumd, bank[7][:, 0:S], V(L, "gb"), None, ALU.add))
                stt(els, cumd, -1.0, cumd, ALU.mult, ALU.min).then_inc(sem("D_abs"), 1)
                e.wait_ge(sem("D_ln"), L + 1)
                ch(stt(lsg, cumd, 0.0, els, ALU.min, ALU.subtract))
                ch(e.tensor_tensor_scan(cumd, C("restart"), lsg, 0.0, ALU.mult, ALU.add))
                c4 = cumd.rearrange("p (c s) -> p c s", s=CHUNK)
                tt(dl.rearrange("p (c s) -> p c s", s=CHUNK), c4[:, :, CHUNK - 1:CHUNK].to_broadcast([P, NCH, CHUNK]),
                   c4, ALU.subtract).then_inc(sem("D_cum"), 1)
                for n in range(2):
                    tt(sqA[:, 2 * n:2 * n + 2, :], qkA[:, 2 * n:2 * n + 2, :], qkA[:, 2 * n:2 * n + 2, :],
                       ALU.mult).then_inc(sem("A_sq"), 1)
                e.wait_ge(sem("D_exp"), 3 * (L + 1))
                ch(stt(qd, qkD[:, 0, :], 32 ** -0.5, eb, ALU.mult, ALU.mult))
                tt(kd, qkD[:, 1, :], enb, ALU.mult)
                tt(kl, qkD[:, 1, :], dl, ALU.mult)
                for q in range(4):
                    ins = ts(qx[:, q, :], qd, C("head32", q, q + 1), None, ALU.mult)
                ins.then_inc(sem("D_qx"), 1)
                for t in range(T):
                    e.wait_ge(sem("D_att"), T * L + t + 1)
                    tt(attD[:, t, :, :], bank[2 + t][:, :].rearrange("p (a c) -> p a c", a=4),
                       over4(C("mask_g", P, 2 * P)), ALU.mult).then_inc(sem("D_atts"), 1)
                for c in range(NCH - 1):
                    e.wait_ge(sem("D_con"), (NCH - 1) * L + c + 1)
                    if c == 0:
                        tt(SD[:, 1, :], bank[5][:, 0:GROUP], C("bd_d"), ALU.mult).then_inc(sem("D_st"), 1)
                    else:
                        e.wait_ge(sem("D_st"), (NCH - 1) * L + c)
                        ch(tt(cm, bank[5 + c][:, 0:GROUP], C("bd_d"), ALU.mult))
                        stt(SD[:, c + 1, :], SD[:, c, :], eb[:, c * CHUNK + CHUNK - 1:(c + 1) * CHUNK], cm,
                            ALU.mult, ALU.add).then_inc(sem("D_st"), 1)
                for i in range(PAIRS):
                    e.wait_ge(sem("D_o"), 2 * L + i + 1)
                    ins = e.tensor_copy(oD[:, i, :], bank[2 + i][:, 0:S])
                ch(ins)
                tt(sqD, oD, oD, ALU.mult).then_inc(sem("D_sq"), 1)
                e.wait_ge(sem("D_rms"), L + 1)
                ch(e.reciprocal(rsD, rsD))
                ch(stt(oD, oD, V(L, "gn_g"), rsD, ALU.mult, ALU.mult))
                e.wait_ge(sem("D_silu"), L + 1)
                tt(yT[:, 6:8, :], oD, sgo, ALU.mult).then_inc(sem("y_D"), 1)
                y_low(L, 1, "y_D", L + 1)
                for n in range(2):
                    e.wait_ge(sem("A_rms"), 2 * L + n + 1)
                    r2 = sqA[:, 2 * n:2 * n + 2, :]
                    ch(e.reciprocal(r2, r2))
                stt(qn, qkA[:, 0:2, :], V(L, "q_g"), sqA[:, 0:2, :], ALU.mult, ALU.mult)
                for m in range(2):
                    ins = stt(kx[:, m], qkA[:, 2:4, :], V(L, f"k_g{m}"), sqA[:, 2:4, :], ALU.mult, ALU.mult)
                ins.then_inc(sem("A_qk"), 1)
                for n, b in enumerate((2, 3, 4, 7)):
                    t, i = n // 2, n % 2
                    kj = P * (t + 1)
                    e.wait_ge(sem("A_s"), 4 * L + n + 1)
                    s, bi = ((s0, bias0), (s1, bias1))[t]
                    ins = stt(s[:, 2 * i:2 * i + 2, :], bank[b][:, 0:2 * kj].rearrange("p (m j) -> p m j", m=2),
                              1.0 / math.sqrt(HD), bi[:, 2 * i:2 * i + 2, :], ALU.mult, ALU.add)
                    if i == 1:
                        ch(ins)
                        mx = negm[:, 4 * t:4 * t + 4]
                        ch(e.tensor_reduce(mx, s, AX_X, ALU.max))
                        ts(mx, mx, -1.0, None, ALU.mult).then_inc(sem("A_max"), 1)
                for t in range(T):
                    e.wait_ge(sem("A_exp"), 8 * L + 4 * t + 4)
                    s = (s0, s1)[t]
                    r4 = rden[:, 4 * t:4 * t + 4]
                    ch(e.reciprocal(r4, den[:, 4 * t:4 * t + 4]))
                    tt(s, s, r4.unsqueeze(2).to_broadcast([P, 4, P * (t + 1)]), ALU.mult).then_inc(sem("A_p"), 1)
                e.wait_ge(sem("A_tr"), 3 * (L + 1))
                e.wait_ge(sem("A_qk"), L + 1)
                e.wait_ge(sem("B_zero"), L + 1)
                e.wait_ge(sem("D_o"), 2 * L + 2)
                ins = e.memset(small[:, 63:64], 0.0)
                ins.then_inc(sem("B_go"), 1)
                e.wait_ge(sem("B_sig"), L + 1)
                ch(tt(hB[:, :, CW - 1:], uB, sgb, ALU.mult))
                for j in range(CW):
                    for i in range(PAIRS):
                        w = V(L, "conv_w", i * CW + j)
                        if j == 0:
                            ins = ts(acc[:, i, :], hB[:, i, 0:S], w, V(L, "conv_b", i), ALU.mult, ALU.add)
                        else:
                            ins = stt(acc[:, i, :], hB[:, i, j:j + S], w, acc[:, i, :], ALU.mult, ALU.add)
                        if j == CW - 1 and i == 1:
                            ins.then_inc(sem("B_acc"), 1)
                        elif i == 1:
                            ch(ins)
                    if j == 15:
                        y_low(L, 2, "y_A", 2 * L + 2)
                e.wait_ge(sem("B_acc"), L + 1)
                e.wait_ge(sem("B_mean"), L + 1)
                ch(tt(xcB, acc, bank[3][:, :].rearrange("p (i s) -> p i s", i=2), ALU.subtract))
                tt(sqB, xcB, xcB, ALU.mult).then_inc(sem("B_xc"), 1)
                e.wait_ge(sem("B_sd"), L + 1)
                ch(e.reciprocal(sqB, sqB))
                ch(tt(xcB, xcB, sqB, ALU.mult))
                for i in range(PAIRS):
                    ins = ts(acc[:, i, :], xcB[:, i, :], V(L, "conv_g", i), V(L, "conv_lb", i), ALU.mult, ALU.add)
                ins.then_inc(sem("B_ln"), 1)
                y_low(L, 3, "y_B", L + 1)
                los(L, 30, 32)
                e.wait_ge(sem("w_used"), unit(L, LAYER_UNITS))
                for n in range(4):
                    c = slice((n % 2) * 512, (n % 2 + 1) * 512)
                    ins = tt(h[:, n // 2, c], h[:, n // 2, c], bank[PROJ[n]][:, :], ALU.add)
                ins.then_inc(sem("h_done"), 1)
                e.wait_ge(sem("h_done"), 2 * L + 1)

            def hidden(j, reg=None):
                e.wait_ge(sem("silu"), at(reg, FB, j + 1))
                if j >= 2:
                    e.wait_ge(sem("ht"), at(reg, FB, j - 1))
                tt(hm[:, j % 2, :], sg[:, j % 2, :], bank[j % 2][:, P:2 * P], ALU.mult).then_inc(sem("hm"), 1)

            def hidden_low(j, reg=None):
                e.wait_ge(sem("hthi"), at(reg, FB, j + 1))
                tt(htlo[:, j % 2, :], bank[2][:, 0:P], hthi[:, j % 2, :].bitcast(F32), ALU.subtract)\
                    .then_inc(sem("htlo"), 1)

            def dense():
                lo(e, DENSE_AT)
                lo(e, DENSE_AT + 1)
                norm(1)
                for b in range(FB):
                    lo(e, DENSE_AT + 3 * b + 2)
                    if b > 0:
                        hidden_low(2 * b - 1)
                    hidden(2 * b)
                    if b < FB - 1:
                        lo(e, DENSE_AT + 3 * b + 3)
                    hidden_low(2 * b)
                    if b < FB - 1:
                        lo(e, DENSE_AT + 3 * b + 4)
                    hidden(2 * b + 1)
                hidden_low(2 * FB - 1)
                wait_down(e, 2 * FB - 1)
                for n in range(4):
                    c = slice((n % 2) * 512, (n % 2 + 1) * 512)
                    ins = tt(h[:, n // 2, c], h[:, n // 2, c], bank[3 + n][:, :], ALU.add)
                ins.then_inc(sem("h_done"), 1)
                e.wait_ge(sem("h_done"), 2)

            def choose(slots, reg, v):
                for t in range(T):
                    s = rkm[:, t, v:v + 1] if reg is None else rkm[:, t, bass.ds(reg + v, 1)]
                    ins = ts(sel[:, t, :], slots, s, None, ALU.is_equal)
                return ins

            def rows_of(k2, reg, v):
                e.wait_ge(sem("M_gath"), at(reg, 2, 2 * v + k2 + 1))
                g = V(1, "ffn_g", 4 * k2, 4).unsqueeze(2).to_broadcast([P, 4, P])
                tt(xgf[:, 4 * k2:4 * k2 + 4, :], bank[5][:, :].rearrange("p (k c) -> p k c", k=4), g, ALU.mult)\
                    .then_inc(sem("M_xgf"), 1)

            def x_low(reg, v):
                for k in range(2):
                    e.wait_ge(sem("M_xhi"), at(reg, 2, 2 * v + k + 1))
                    tt(xlo[:, 4 * k:4 * k + 4, 0:P], xgf[:, 4 * k:4 * k + 4, :],
                       xhi[:, 4 * k:4 * k + 4, 0:P].bitcast(F32), ALU.subtract).then_inc(sem("M_xlo"), 1)

            def experts(again, first, j0):
                slots = C("iota", P * again, P * again + P)
                v0 = (NE + 1) * again
                if again:
                    e.wait_ge(sem("M_gath"), 2 * v0)
                choose(slots, None, 0).then_inc(sem("M_sel"), 1)
                lo(e, first)
                lo(e, first + 1)
                if again:
                    e.wait_ge(sem("M_xlo"), 2 * v0)
                rows_of(0, None, v0)
                rows_of(1, None, v0)
                e.wait_ge(sem("M_xgf"), 2 * v0 + 2)
                x_low(None, v0)
                with e.Fori(0, NE) as ex:
                    for b in range(FB):
                        j, u = j0 + b, first + 2 + 3 * b
                        lo(e, u, ex)
                        if b > 0:
                            hidden_low(j - 1, ex)
                        lo(e, u + 1, ex)
                        lo(e, u + 2, ex)
                        if b == 2:
                            for t in range(T):
                                ins = ts(selg[:, t, :], slots, rkm[:, t, bass.ds(ex, 1)], gat[:, t, bass.ds(ex, 1)],
                                         ALU.is_equal, ALU.mult)
                            ins.then_inc(sem("M_selg"), 1)
                        if b == 4:
                            e.wait_ge(sem("M_gath"), ex * 2 + (2 * v0 + 2))
                            choose(slots, ex, 1).then_inc(sem("M_sel"), 1)
                        if b == 9:
                            e.wait_ge(sem("M_xlo"), ex * 2 + (2 * v0 + 2))
                            rows_of(0, ex, v0 + 1)
                        if b == 13:
                            rows_of(1, ex, v0 + 1)
                        hidden(j, ex)
                    hidden_low(j0 + FB - 1, ex)
                    x_low(ex, v0 + 1)
                    for n in range(4):
                        t, c = n // 2, slice((n % 2) * 512, (n % 2 + 1) * 512)
                        e.wait_ge(sem("M_comb"), ex * 4 + (4 * NE * again + n + 1))
                        tt(h[:, t, c], h[:, t, c], bank[6 + n % 2][:, :], ALU.add).then_inc(sem("M_add"), 1)
                    e.wait_ge(sem("M_add"), ex * 4 + (4 * NE * again + 4))
                e.memset(small[:, 62:63], 0.0).then_inc(sem("h_done"), 1)

            def route():
                for t in range(T):
                    e.wait_ge(sem("R_lg"), t + 1)
                    ins = e.tensor_copy(lg[:, t, :], bank[6 + t][:, 0:NE])
                ch(ins)
                for t in range(T):
                    ins = e.max(top[:, t, :], lg[:, t, :])
                ch(ins)
                for t in range(T):
                    ins = e.max_index(idx[:, t, :], top[:, t, :], lg[:, t, :])
                ch(ins)
                ch(e.tensor_copy(idxf, idx[:]))
                for t in range(T):
                    for q, dst in enumerate((e1, e2)):
                        ins = ts(dst[:, t, :], C("iota8"), idxf[:, t, q:q + 1], None, ALU.is_equal)
                ch(ins)
                tt(mk, e1, e2, ALU.add).then_inc(sem("R_mk"), 1)
                tt(dif, top[:, :, 1:2], top[:, :, 0:1], ALU.subtract).then_inc(sem("R_dif"), 1)
                e.wait_ge(sem("R_exp"), 1)
                ch(ts(ga, dif, 1.0, None, ALU.add))
                ch(e.reciprocal(ga, ga))
                ch(tt(gb_, ga, dif, ALU.mult))
                for t in range(T):
                    ins = ts(gat[:, t, :], e1[:, t, :], ga[:, t, :], None, ALU.mult)
                ch(ins)
                for t in range(T):
                    ins = stt(gat[:, t, :], e2[:, t, :], gb_[:, t, :], gat[:, t, :], ALU.mult, ALU.add)
                ch(ins)
                e.wait_ge(sem("R_rank"), 1)
                ch(e.memset(rkm, -1.0))
                ch(stt(rkm[:, :, 0:NE], bank[2][:, 0:16].rearrange("p (t e) -> p t e", t=T), 1.0, mk,
                       ALU.add, ALU.mult))
                ch(ts(rkm[:, :, 0:NE], rkm[:, :, 0:NE], 1.0, None, ALU.subtract))
                ch(e.tensor_reduce(small[:, 4:5], bank[2][:, 16:24], AX_X, ALU.max))
                e.tensor_copy(over[:], small[:, 4:5]).then_inc(sem("R_over"), 1)
                e.wait_ge(sem("R_over"), 1)

            e.wait_ge(sem("con_in"), 80)
            if stop >= 1:
                mixers(0)
            if stop >= 2:
                dense()
            if stop >= 3:
                mixers(1)
            if stop >= 4:
                norm(3, split=False)
                route()
                experts(0, MOE_AT, 2 * FB)
                with e.If(e.value_load(over[0:1, 0:1], min_val=0, max_val=S) > P):
                    experts(1, AGAIN_AT, 2 * FB + NE * FB)


def lay_out(i):
    f = np.float32
    x = np.asarray(i["x"], f).reshape(S, D)

    def cols(a):
        return np.asarray(a, f).reshape(-1, P).T

    vec = np.zeros((P, LAYERS, NV), f)
    for L in range(LAYERS):
        def put(name, a):
            o, n = VEC[name]
            vec[:, L, o:o + n] = a

        def twice(a):
            return np.concatenate([a, a])[:, None]

        put("mix_g", cols(i["mix_norm_g"][L]))
        put("ffn_g", cols(i["ffn_norm_g"][L]))
        put("q_g", twice(i["attn_q_norm_g"][L]))
        z = np.zeros(HD, f)
        put("k_g0", np.concatenate([i["attn_k_norm_g"][L], z])[:, None])
        put("k_g1", np.concatenate([z, i["attn_k_norm_g"][L]])[:, None])
        put("conv_w", np.asarray(i["conv_w"][L], f).T.reshape(PAIRS, P, CW).transpose(1, 0, 2).reshape(P, -1))
        for name, key in (("conv_b", "conv_b"), ("conv_g", "conv_ln_g"), ("conv_lb", "conv_ln_b"), ("mu", "rwkv_mu"),
                          ("w0", "rwkv_w0"), ("a0", "rwkv_a0"), ("k_k", "rwkv_k_k"), ("k_a", "rwkv_k_a"),
                          ("r_k", "rwkv_r_k"), ("ln_g", "rwkv_ln_g"), ("ln_b", "rwkv_ln_b"), ("gb", "gla_gb")):
            put(name, cols(i[key][L]))
        put("gn_g", twice(i["gla_norm_g"][L]))
    lora = np.zeros((P, LAYERS, 3, GROUP), f)
    for L in range(LAYERS):
        lora[0:32, L, 0] = i["rwkv_w2"][L]
        lora[32:64, L, 1] = i["rwkv_a2"][L]
        lora[64:128, L, 2] = i["rwkv_g2"][L]
    gla2 = np.ascontiguousarray(np.asarray(i["gla_g2"], f).transpose(1, 0, 2))
    router = np.ascontiguousarray(np.asarray(i["moe_router"][0], f).reshape(KD, P, NE).transpose(1, 0, 2))

    wst = np.zeros((MAIN_UNITS, P, UC), f)

    def w_in(at, L):
        w = np.asarray(i["w_in"][L], f).reshape(KD, P, -1)
        for u, (c, n) in enumerate(Z_COLS):
            wst[at + u].reshape(P, KD, P)[:, :, :n] = w[:, :, c:c + n].transpose(1, 0, 2)

    def w_out(at, L):
        w = np.asarray(i["w_out"][L], f).reshape(KD, P, D)
        for u, k in enumerate((4, 5, 6, 7, 0, 1, 2, 3)):
            wst[at + u] = w[k]

    def gate_up(at, wg, wu, b):
        g = wg.reshape(KD, P, FF)[:, :, b * P:(b + 1) * P]
        u = wu.reshape(KD, P, FF)[:, :, b * P:(b + 1) * P]
        gu = np.concatenate([g, u], 2).transpose(1, 0, 2)
        wst[at] = gu[:, :4].reshape(P, UC)
        wst[at + 1] = gu[:, 4:].reshape(P, UC)

    for L in range(LAYERS):
        base = 0 if L == 0 else LAYER1_AT
        w_in(base, L)
        w_out(base + Z_UNITS, L)
    wg, wu, wd = (np.asarray(i[k][0], f) for k in ("ffn_wg", "ffn_wu", "ffn_wd"))
    for b in range(FB):
        gate_up(DENSE_AT + 3 * b, wg, wu, b)
        wst[DENSE_AT + 3 * b + 2] = wd[b * P:(b + 1) * P]
    for ex in range(NE):
        wg, wu, wd = (np.asarray(i[k][0][ex], f) for k in ("moe_wg", "moe_wu", "moe_wd"))
        at_ = MOE_AT + ex * F_UNITS
        for b in range(FB):
            gate_up(at_ + (0 if b == 0 else 2 + 3 * (b - 1)), wg, wu, b)
            wst[at_ + 2 + 3 * b + (2 if b < FB - 1 else 0)] = wd[b * P:(b + 1) * P]
    return {"x": x, "cons": constants(), "vecs": vec, "lora": lora, "gla2": gla2, "router": router,
            "relb": np.repeat(np.asarray(i["rel_bias"], f)[:, :, None], P, 2), "wst": wst}


PROJ = (0, 1, 5, 6)


def kernel(**inputs):
    import concourse.bacc as bacc
    from concourse.bass_utils import run_bass_kernel_spmd

    nc = bacc.Bacc("TRN2", target_bir_lowering=False, num_devices=1)
    arrays = lay_out({k: np.asarray(v) for k, v in inputs.items()})
    args = [nc.dram_tensor(f"in_{n}", a.shape, mybir.dt.from_np(a.dtype), kind="ExternalInput").ap()
            for n, a in arrays.items()]
    out = nc.dram_tensor("out_h", (S, D), F32, kind="ExternalOutput").ap()
    build(nc, *args, out)
    r = run_bass_kernel_spmd(nc, [{f"in_{n}": a for n, a in arrays.items()}], core_ids=[0])
    return r.results[0]["out_h"].reshape(1, S, D)
```

```python
from contextlib import ExitStack
import math

import numpy as np
import concourse.bass as bass
import concourse.mybir as mybir

ALU = mybir.AluOpType
ACT = mybir.ActivationFunctionType
AX_X = mybir.AxisListType.X
F32 = mybir.dt.float32
F32R = mybir.dt.float32r
U32 = mybir.dt.uint32
I32 = mybir.dt.int32

P = 128
D = 1024
S = 256
LAYERS = 2
T = S // P
KD = D // P
GROUP = 256
PAIRS = GROUP // P
HD = 64
CW = 31
CHUNK = 64
NCH = S // CHUNK
FF = 2816
FB = FF // P
NE = 8
EPS = 1e-6
LEVELS = 6
KAPPA = math.exp(-0.5)

UC = 1024
RAW = 3
RING = 6
HELD = 6
Z_UNITS = 24
O_UNITS = 8
F_UNITS = 3 * FB
LAYER_UNITS = Z_UNITS + O_UNITS
DENSE_AT = LAYER_UNITS
LAYER1_AT = DENSE_AT + F_UNITS
MOE_AT = LAYER1_AT + LAYER_UNITS
AHEAD = 3
PAD = 6
MAIN_UNITS = MOE_AT + NE * F_UNITS + PAD
AGAIN_AT = MAIN_UNITS
assert F_UNITS % HELD == 0 and F_UNITS % RING == 0 and RING == 2 * RAW

_A, _B, _C, _D = 0, 768, 1280, 2176
Z_COLS = [(_C + 128 * i, 128) for i in range(7)]
Z_COLS += [(_B + 128 * i, 128) for i in range(4)]
Z_COLS += [(_D, 128), (_D + 128, 128), (_D + 256, 128), (_D + 384, 128), (_D + 512, 16),
           (_D + 528, 128), (_D + 656, 128)]
Z_COLS += [(_A + 128 * i, 128) for i in range(6)]
assert len(Z_COLS) == Z_UNITS
UB0, UD0, UA0 = 7, 11, 18
V_UNITS = (UD0 + 2, UA0 + 4)
Y_CHUNK = (4, 2, 6, 0)

PROJ = (0, 1, 5, 6)

VEC = {}
for _name, _n in (("mix_g", 8), ("ffn_g", 8), ("q_g", 1), ("k_g0", 1), ("k_g1", 1), ("conv_w", 2 * CW),
                  ("conv_b", 2), ("conv_g", 2), ("conv_lb", 2), ("mu", 7), ("w0", 2), ("a0", 2), ("k_k", 2),
                  ("k_a", 2), ("r_k", 2), ("ln_g", 2), ("ln_b", 2), ("gb", 1), ("gn_g", 1)):
    VEC[_name] = (sum(n for _, n in VEC.values()), _n)
NV = sum(n for _, n in VEC.values())

CON = {}
for _name, _n in (("ident", P), ("eps", 3), ("blk", P), ("lvl", LEVELS * P), ("mask_g", 4 * P), ("logm", 3 * P),
                  ("upper", P), ("ones", P), ("iota", 2 * P), ("restart", S), ("iota8", 8),
                  ("head32", 4), ("bd_d", 2 * P), ("buckets", 3 * P)):
    CON[_name] = (sum(n for _, n in CON.values()), _n)
NC_ = sum(n for _, n in CON.values())
NCON = CON["buckets"][0]

FIRST = CON["blk"][0]

NEG = -1e30


def t5_bucket(dist):
    n = np.maximum(dist, 0)
    large = 16 + (np.log(np.maximum(n, 1) / 16) / math.log(2048 / 16) * 16).astype(np.int32)
    return np.where(n < 16, n, np.minimum(large, 31)).astype(np.int32)


def constants():
    c = np.zeros((P, NC_), np.float32)

    def put(name, a):
        o, n = CON[name]
        c[:a.shape[0], o:o + n] = a.reshape(a.shape[0], -1)

    r, q = np.arange(P)[:, None], np.arange(P)[None, :]
    put("ident", np.eye(P, dtype=np.float32))
    put("blk", (r // HD == q // HD) / HD)
    lv = [(r // (2 << l) == q // (2 << l)) & ((r >> l) % 2 == 1) & ((q >> l) % 2 == 0) for l in range(LEVELS)]
    put("lvl", np.stack(lv, 1).astype(np.float32))
    same = r // CHUNK == q // CHUNK
    su, iu = same & (r < q), same & (r <= q)
    put("mask_g", np.stack([su, iu, su, iu], 1).astype(np.float32))
    cols = []
    for t0, j0 in ((0, 0), (128, 0), (128, 128)):
        d = (t0 + r) - (j0 + q)
        m = ((d >= 0) & (d <= 128)).astype(int) + ((d >= 0) & (d % 4 == 0)) + ((d >= 0) & (d % 16 == 0))
        cols.append(np.where(m > 0, np.log(np.maximum(m, 1)), NEG))
    put("logm", np.stack(cols, 1).astype(np.float32))
    put("upper", (r < q).astype(np.float32))
    put("ones", np.ones((P, P), np.float32))
    put("iota", np.broadcast_to(np.arange(2 * P), (P, 2 * P)))
    put("restart", np.broadcast_to((np.arange(S) % CHUNK != 0), (P, S)).astype(np.float32))
    put("iota8", np.broadcast_to(np.arange(8), (P, 8)))
    put("eps", np.broadcast_to(np.array([EPS, 64e-5, 1e-5]), (P, 3)))
    put("head32", (r // 32 == np.arange(4)[None, :]).astype(np.float32))
    put("bd_d", (r // 32 == np.arange(2 * P)[None, :] // HD).astype(np.float32))
    y = np.arange(3 * P)[None, :]
    dist = (S - 1) - y
    put("buckets", ((np.arange(32)[:, None] == t5_bucket(dist)) & (dist >= 0)).astype(np.float32))
    return c


class Chain:

    def __init__(self, eng, sem):
        self.eng, self.sem, self.n, self.base, self.reg, self.per = eng, sem, 0, 0, None, 0

    def loop(self, reg, per):
        self.base, self.n, self.reg, self.per = self.n, 0, reg, per

    def end_loop(self, times):
        assert self.n == self.per, (self.n, self.per)
        self.n, self.reg = self.base + self.per * times, None

    def value(self):
        return self.n if self.reg is None else self.reg * self.per + (self.base + self.n)

    def __call__(self, ins):
        self.n += 1
        ins.then_inc(self.sem, 1)
        self.eng.wait_ge(self.sem, self.value())


class Area:

    def __init__(self, tensor, at=0, end=None):
        self.tensor, self.at, self.end = tensor, at, end or tensor.shape[1]

    def __call__(self, *shape):
        n = int(np.prod(shape))
        v = self.tensor[:, self.at:self.at + n]
        self.at += n
        assert self.at <= self.end, (self.at, self.end)
        if len(shape) > 1:
            names = "abcde"[:len(shape)]
            sizes = {k: s for k, s in zip(names[1:], shape[1:])}
            v = v.rearrange("p (" + " ".join(names) + ") -> p " + " ".join(names), **sizes)
        return v


def build(nc, x, cons, vecs, lora, gla2, router, relb, wst, out):
    ctx = ExitStack()
    with ctx:
        def sb(name, shape, dt=F32):
            return ctx.enter_context(nc.sbuf_tensor(name, shape, dt))

        sems = {}

        def sem(name):
            if name not in sems:
                sems[name] = ctx.enter_context(nc.semaphore(name))
            return sems[name]

        bank = [ctx.enter_context(nc.psum_tensor(f"bank{i}", [P, 512], F32)) for i in range(8)]

        h = sb("h", [P, T, D])
        xsq = sb("xsq", [P, T * D])
        xnf = sb("xnf", [P, KD, S])
        xhi = sb("xhi", [P, KD, S], F32R)
        xlo = sb("xlo", [P, KD, S], F32R)
        raw = sb("raw", [P, RAW, UC])
        whi = sb("whi", [P, HELD, UC], F32R)
        wlo = sb("wlo", [P, HELD, UC], F32R)
        con = sb("con", [P, NCON])
        vec = sb("vec", [P, LAYERS, NV])
        lor = sb("lor", [P, LAYERS, 3, GROUP])
        g2s = sb("g2s", [16, LAYERS, P])
        rou = sb("rou", [P, KD, NE])
        rel = sb("rel", [32, 4, P])
        bias0 = sb("bias0", [P, 4, P])
        bias1 = sb("bias1", [P, 4, S])
        small = sb("small", [P, 64])
        tap = sb("tap", [P, PAIRS, S])
        idx = sb("idx", [P, T, 8], U32)
        over = sb("over", [P, 1], I32)
        hthi = sb("hthi", [P, 2, P], F32R)
        htlo = sb("htlo", [P, 2, P], F32R)
        selt = sb("selt", [P, T, P], F32R)
        arena = sb("arena", [P, 18256])
        ext_dram = nc.dram_tensor("ext_dram", [P, 4, 3 * P], F32, kind="Internal").ap()
        xs = xsq[:, :].rearrange("p (t d) -> p t d", t=T)
        yT = xnf
        ssq, rstd, cnt = small[:, 0:2], small[:, 2:4], small[:, 4:5]
        negm, den, rden = small[:, 8:16], small[:, 16:24], small[:, 24:32]

        def C(name, a=0, b=None):
            o, n = CON[name]
            return con[:, o + a:o + (n if b is None else b)]

        def V(L, name, i=0, n=1):
            return vec[:, L, VEC[name][0] + i:VEC[name][0] + i + n]

        blk, ident = C("blk"), C("ident")

        def over4(a):
            return a.unsqueeze(1).to_broadcast([P, 4, P])

        ax = Area(xsq)
        qkA, vA, gB = ax(4, S), ax(T, GROUP), ax(2, S)
        ar = Area(arena)
        zC = ar(7, S + 1)
        X, BVs = Area(arena)(8, P), Area(arena, 8 * P)(T, PAIRS, 2, HD)
        XA = Area(arena)(T * PAIRS, P)
        qkD, vD, gdD, ogD = ar(2, S), ar(T, GROUP), ar(S), ar(2, S)
        uB, hB = ar(2, S), ar(2, S + CW - 1)
        free_at = ar.at
        zs = ar(7, S)
        st_at = ar.at
        lin, sgw, sga = ar(S), ar(PAIRS, S), ar(PAIRS, S)
        ST = Area(arena, st_at)(NCH, PAIRS, P)
        gC, bonus = ar(PAIRS, S), ar(PAIRS, S)
        cum_at = ar.at
        cum, cinv, kkn, knew = ar(PAIRS, S), ar(PAIRS, S), ar(PAIRS, S), ar(PAIRS, S)
        ca = Area(arena, cum_at)
        khtok, betok, Ws, Us = ca(T, GROUP), ca(T, GROUP), ca(T, PAIRS, P), ca(T, PAIRS, P)
        alr = ar(2, PAIRS, S)
        sq_at = ar.at
        sq = ar(PAIRS, S)
        altok = Area(arena, sq_at)(T, GROUP)
        cend = ar(PAIRS, NCH)
        vtok = ar(T, GROUP)
        mats_at = ar.at
        mats = ar(8, 4, P)
        XT = ar(8, P)
        stc = ar(PAIRS, P)
        yC = sq
        yc2 = Area(arena, cum_at)(PAIRS, S)

        ad = Area(arena, free_at)
        els, cumd, lsg = ad(S), ad(S), ad(S)
        qx = Area(arena, free_at)(4, S)
        ad = Area(arena, free_at + 4 * S)
        dl, eb, enb = ad(S), ad(S), ad(S)
        qd, kd, kl = qkD[:, 0, :], enb, dl
        attD = Area(arena, st_at)(T, 4, P)
        ad = Area(arena, mats_at)
        kltok, SD, cm = ad(T, P), ad(NCH, GROUP), ad(GROUP)
        oD, sqD, rsD, sgo = ad(PAIRS, S), ad(PAIRS, S), ad(PAIRS, S), ad(PAIRS, S)
        aa = Area(arena, cum_at + 2 * S)
        sqA, qn, kx = aa(4, S), aa(PAIRS, S), aa(2, PAIRS, S)
        assert aa.at <= sq_at and ad.at <= mats_at + 32 * P
        aa = Area(arena, free_at)
        s0, s1 = aa(4, P), aa(4, S)
        pt = Area(arena, st_at)(12, P)
        acc, sqB = uB, hB[:, :, 0:S]

        am = Area(arena)
        xgf, sel = am(KD, P), am(T, P)
        sg, hm = am(2, P), am(2, P)
        scaled = am(4, 512)
        rkm, gat = am(T, NE + 1), am(T, NE)
        lg, top, idxf, e1, e2, mk = am(T, NE), am(T, 8), am(T, 8), am(T, NE), am(T, NE), am(T, NE)
        dif, ga, gb_ = am(T, 1), am(T, 1), am(T, 1)
        gate = am(T, 1)
        aext = Area(arena, mats_at)
        bkt, ext = aext(3 * P), aext(4, 3 * P)

        more_raw = Area(arena, arena.shape[1] - RAW * UC)(RAW, UC)

        def place(n, mixer=False):
            if mixer:
                return raw[:, n % RAW, :]
            return (raw if n % RING < RAW else more_raw)[:, n % RAW, :]

        def landing(n, reg=None):
            mixer = reg is None and (n < DENSE_AT or LAYER1_AT <= n < MOE_AT)
            return place(n, mixer)

        def unit(L, u):
            return (0 if L == 0 else LAYER1_AT) + u

        def z_at(u):
            if u < UB0:
                return zC[:, u, 1:S + 1], False
            if u < UD0:
                v = u - UB0
                return [uB, gB][v // 2][:, v % 2, :], False
            if u < UA0:
                v = u - UD0
                return [qkD[:, 0, :], qkD[:, 1, :], vD, None, gdD, ogD[:, 0, :],
                        ogD[:, 1, :]][v], v in (2, 3)
            v = u - UA0
            return (qkA[:, v, :], False) if v < 4 else (vA, True)

        def con_D(c):
            return (bank[7][:, 0:GROUP], bank[2][:, GROUP:], bank[7][:, GROUP:])[c]

        def at(reg, per, v):
            return v if reg is None else reg * per + v

        def hi(e, n, reg=None):
            e.wait_ge(sem(f"raw_in{n % RING}"), at(reg, 16 * F_UNITS // RING, 16 * (n // RING + 1)))
            if n >= HELD:
                e.wait_ge(sem("w_used"), at(reg, F_UNITS, n - HELD + 1))
            e.activation(whi[:, n % HELD, :], landing(n, reg), ACT.Copy).then_inc(sem("w_high"), 1)

        def lo(e, n, reg=None):
            e.wait_ge(sem("w_high"), at(reg, F_UNITS, n + 1))
            e.tensor_tensor(wlo[:, n % HELD, :], landing(n, reg), whi[:, n % HELD, :].bitcast(F32),
                            ALU.subtract).then_inc(sem("w_split"), 1)

        def gu_unit(b):
            return 0 if b == 0 else 2 + 3 * (b - 1)

        def wd_unit(b):
            return 2 + 3 * b + (2 if b < FB - 1 else 0)

        def wait_gate_up(e, j, first=None, reg=None):
            if first is not None:
                b = (j - 2 * FB) % FB
                e.wait_ge(sem("w_used"), at(reg, F_UNITS, first + gu_unit(b) + 2))
            elif j % 2 == 0:
                e.wait_ge(sem("gu"), j // 2 + 1)
            else:
                e.wait_ge(sem("w_used"), DENSE_AT + 3 * (j // 2) + 2)

        def wait_down(e, j, first=None, reg=None, before=0):
            if first is not None:
                b = (j - 2 * FB) % FB - before
                n = first + wd_unit(b % FB) + 1 - (F_UNITS if b < 0 else 0)
                e.wait_ge(sem("w_used"), at(reg, F_UNITS, n))
            elif (j - before) % 2 == 0:
                e.wait_ge(sem("down"), (j - before) // 2 + 1)
            else:
                e.wait_ge(sem("w_used"), DENSE_AT + 3 * ((j - before) // 2) + 3)

        COMBINE = (6, 7, 5, 3)

        def y_part(x_, half):
            return x_[:, 4 * half:4 * half + 4, P:S]

        def y_psum(half):
            return bank[3 + half][:, :].rearrange("p (a c) -> p a c", a=4)

        def choose(e, slots, reg, v):
            for t in range(T):
                s = rkm[:, t, v:v + 1] if reg is None else rkm[:, t, bass.ds(reg + v, 1)]
                ins = e.tensor_scalar(sel[:, t, :], slots, s, None,
                                      ALU.is_equal)
            return ins

        def rows_of(e, k2, reg, v):
            e.wait_ge(sem("M_gath"), at(reg, 2, 2 * v + k2 + 1))
            g = V(1, "ffn_g", 4 * k2, 4).unsqueeze(2).to_broadcast([P, 4, P])
            e.tensor_tensor(xgf[:, 4 * k2:4 * k2 + 4, :], bank[5 + k2][:, :].rearrange("p (k c) -> p k c", k=4), g, ALU.mult)\
                .then_inc(sem("M_xgf"), 1)

        def rows_low(e, k, reg, v):
            e.wait_ge(sem("M_xhi"), at(reg, 2, 2 * v + k + 1))
            e.tensor_tensor(xlo[:, 4 * k:4 * k + 4, 0:P], xgf[:, 4 * k:4 * k + 4, :],
                            xhi[:, 4 * k:4 * k + 4, 0:P].bitcast(F32), ALU.subtract).then_inc(sem("M_xlo"), 1)

        block = ctx.enter_context(nc.Block())

        @block.sync
        def _(sp):
            sp.dma_start(h[:], x.rearrange("(t p) d -> p t d", p=P)).then_inc(sem("x_in"), 16)
            sp.dma_start(con[:, 0:FIRST], cons[:, 0:FIRST]).then_inc(sem("con_in"), 16)
            sp.dma_start(vec[:], vecs).then_inc(sem("con_in"), 16)
            for n in range(RAW):
                sp.dma_start(raw[:, n, :], wst[n]).then_inc(sem(f"raw_in{n}"), 16)
            sp.dma_start(con[:, FIRST:], cons[:, FIRST:NCON]).then_inc(sem("con2_in"), 16)
            sp.dma_start(lor[:], lora).then_inc(sem("con2_in"), 16)
            sp.dma_start(g2s[:], gla2).then_inc(sem("con2_in"), 16)
            sp.dma_start(rou[:], router).then_inc(sem("con2_in"), 16)
            o, n = CON["buckets"]
            sp.dma_start(bkt, cons[:, o:o + n]).then_inc(sem("ext_in"), 16)
            sp.dma_start(rel[:], relb).then_inc(sem("ext_in"), 16)

            def stream(first, count, depth, source, mixer=False):
                with sp.Fori(0, count // RING) as r:
                    for i in range(RING):
                        n = first + i
                        sp.wait_ge(sem("w_split"), r * RING + (n + 1 - depth))
                        sp.dma_start(place(n, mixer),
                                     wst[bass.ds(r * RING + (source + i), 1)].rearrange("a p c -> p (a c)"))\
                          .then_inc(sem(f"raw_in{n % RING}"), 16)
                for i in range(count // RING * RING, count):
                    n = first + i
                    sp.wait_ge(sem("w_split"), n + 1 - depth)
                    sp.dma_start(place(n, mixer), wst[source + i]).then_inc(sem(f"raw_in{n % RING}"), 16)

            stream(RAW, DENSE_AT - RAW, RAW, RAW, True)
            sp.wait_ge(sem("y_D"), 1)
            stream(DENSE_AT, RING, RAW, DENSE_AT)
            stream(DENSE_AT + RING, F_UNITS - RING, RING, DENSE_AT + RING)
            stream(LAYER1_AT, LAYER_UNITS, RAW, LAYER1_AT, True)
            sp.wait_ge(sem("y_D"), 2)
            stream(MOE_AT, RING, RAW, MOE_AT)
            stream(MOE_AT + RING, NE * F_UNITS + PAD - RING, RING, MOE_AT + RING)
            sp.wait_ge(sem("h_done"), 4)
            with sp.If(sp.value_load(over[0:1, 0:1], min_val=0, max_val=S) > P):
                stream(AGAIN_AT, NE * F_UNITS + PAD, RING, MOE_AT)
                sp.wait_ge(sem("h_done"), 5)
            sp.dma_start(out.rearrange("(t p) d -> p t d", p=P), h[:]).then_inc(sem("stored"), 16)
            sp.wait_ge(sem("stored"), 16)

        @block.scalar
        def _(e):
            act = e.activation

            def norm(n, split=True, units=((), ())):
                if n == 0:
                    e.wait_ge(sem("con_in"), 32)
                act(small[:, 63:64], C("eps", 0, 1), ACT.Sqrt)
                for t in range(T):
                    if n == 0:
                        e.wait_ge(sem("x_in"), 16)
                    else:
                        e.wait_ge(sem("h_first"), n) if t == 0 else e.wait_ge(sem("h_done"), n)
                    act(xs[:, t, :], h[:, t, :], ACT.Square, accum_out=ssq[:, t:t + 1]).then_inc(sem("ssq"), 1)
                e.wait_ge(sem("ssq"), T * (n + 1))
                act(rstd, ssq, ACT.Sqrt, scale=1.0 / D, bias=C("eps", 0, 1)).then_inc(sem("rms"), 1)
                for u in units[0]:
                    hi(e, u)
                for j in range(4 if split else 0):
                    e.wait_ge(sem("xnf"), 4 * n + j + 1)
                    act(xhi[:, 2 * j:2 * j + 2, :], xnf[:, 2 * j:2 * j + 2, :], ACT.Copy).then_inc(sem("xhi"), 1)
                for u in units[1]:
                    hi(e, u)

            def z_evac(L, u):
                if u - 1 in V_UNITS:
                    return
                dst, rows = z_at(u)
                e.wait_ge(sem("w_used"), unit(L, u) + (2 if rows else 1))
                src = bank[u % 2]
                act(dst, src[:, :].rearrange("p (t c) -> p t c", t=T) if rows else src[:, 0:S], ACT.Copy)\
                    .then_inc(sem("z_out"), 2 if rows else 1)

            def zs_upto(L, a, b):
                for u in range(a, b):
                    z_evac(L, u)
                    hi(e, unit(L, u + HELD))

            def y_high(L, j, name, n):
                e.wait_ge(sem(name), n)
                if j == 0:
                    e.wait_ge(sem("w_used"), unit(L, Z_UNITS))
                k = Y_CHUNK[j]
                act(xhi[:, k:k + 2, :], yT[:, k:k + 2, :], ACT.Copy).then_inc(sem("yhi"), 1)

            def bias():
                e.wait_ge(sem("ext_mm"), 1)
                for hh in range(4):
                    act(ext[:, hh, :], bank[2 + hh][:, 0:3 * P], ACT.Copy).then_inc(sem("ext_sb"), 1)

            def mixers(L):
                if L > 0:
                    hi(e, unit(L, 0))
                norm(2 * L, units=([unit(L, u) for u in (0, 1, 2)[L:]], [unit(L, 3)]))
                for u in range(2):
                    z_evac(L, u)
                    hi(e, unit(L, 4 + u))
                for u in range(HELD, HELD + 2):
                    hi(e, unit(L, u))
                if L == 0:
                    bias()
                zs_upto(L, 2, 7)
                zs_upto(L, 7, 9)
                e.wait_ge(sem("C_shift"), L + 1)
                act(lin[0:32, :], zs[0:32, 6, :], ACT.Tanh).then_inc(sem("C_lin"), 1)
                act(lin[32:64, :], zs[32:64, 6, :], ACT.Copy).then_inc(sem("C_lin"), 1)
                act(lin[64:128, :], zs[64:128, 6, :], ACT.Sigmoid).then_inc(sem("C_lin"), 1)
                e.wait_ge(sem("C_lora"), L + 1)
                for i in range(PAIRS):
                    act(sga[:, i, :], bank[3][:, i * S:(i + 1) * S], ACT.Sigmoid, bias=V(L, "a0", i))\
                        .then_inc(sem("C_sga"), 1)
                for i in range(PAIRS):
                    act(sgw[:, i, :], bank[2][:, i * S:(i + 1) * S], ACT.Sigmoid, bias=V(L, "w0", i))\
                        .then_inc(sem("C_sgw"), 1)
                act(gC, bank[4][:, :].rearrange("p (i s) -> p i s", i=PAIRS), ACT.Copy).then_inc(sem("C_g"), 1)
                zs_upto(L, 9, 11)
                e.wait_ge(sem("z_out"), Z_UNITS * L + UD0)
                act(gB, gB, ACT.Sigmoid).then_inc(sem("B_sig"), 1)
                e.wait_ge(sem("C_kmax"), L + 1)
                act(sq, sq, ACT.Ln, scale=float(HD)).then_inc(sem("C_kln"), 1)
                zs_upto(L, 11, 12)
                e.wait_ge(sem("C_kln"), L + 1)
                act(sq, sq, ACT.Exp, scale=-0.5).then_inc(sem("C_kn"), 1)
                e.wait_ge(sem("C_cum"), L + 1)
                act(cinv, cum, ACT.Exp, scale=KAPPA).then_inc(sem("C_exp"), 1)
                act(sgw, sgw, ACT.Exp, scale=-KAPPA).then_inc(sem("C_exp"), 1)
                act(alr[:, 1], cum, ACT.Exp, scale=-KAPPA).then_inc(sem("C_exp"), 1)
                z_evac(L, 12)
                e.wait_ge(sem("C_exp"), 3 * (L + 1))
                for n, dst in enumerate((vtok, khtok, altok, betok)):
                    e.wait_ge(sem("C_tr"), 4 * L + n + 1)
                    act(dst, bank[2 + n][:, :].rearrange("p (t c) -> p t c", t=T), ACT.Copy)\
                        .then_inc(sem("C_tok"), 1)
                hi(e, unit(L, 12 + HELD))
                zs_upto(L, 13, 16)
                e.wait_ge(sem("C_bv"), L + 1)
                act(BVs, bank[2][:, :].rearrange("p (t i m v) -> p t i m v", t=T, i=PAIRS, m=2), ACT.Copy)\
                    .then_inc(sem("C_bvs"), 1)
                e.wait_ge(sem("D_abs"), L + 1)
                act(els, els, ACT.Exp).then_inc(sem("D_e"), 1)
                e.wait_ge(sem("D_e"), L + 1)
                act(els, els, ACT.Ln, bias=1.0).then_inc(sem("D_ln"), 1)
                zs_upto(L, 16, 17)
                e.wait_ge(sem("D_cum"), L + 1)
                act(eb, cumd, ACT.Exp, scale=1.0 / 16).then_inc(sem("D_exp"), 1)
                act(enb, cumd, ACT.Exp, scale=-1.0 / 16).then_inc(sem("D_exp"), 1)
                act(dl, dl, ACT.Exp, scale=1.0 / 16).then_inc(sem("D_exp"), 1)
                zs_upto(L, 17, 21)
                z_evac(L, 21)
                e.wait_ge(sem("C_w"), L + 1)
                act(Ws, bank[3][:, :].rearrange("p (t i v) -> p t i v", t=T, i=PAIRS), ACT.Copy)\
                    .then_inc(sem("C_ws"), 1)
                e.wait_ge(sem("C_xa"), L + 1)
                act(XA, bank[4][:, :].rearrange("p (a c) -> p a c", a=4), ACT.Copy).then_inc(sem("C_xas"), 1)
                hi(e, unit(L, 21 + HELD))
                zs_upto(L, 22, 24)
                e.wait_ge(sem("C_var"), L + 1)
                act(yc2, bank[6][:, :].rearrange("p (i s) -> p i s", i=2), ACT.Ln, bias=C("eps", 1, 2))\
                    .then_inc(sem("C_ln"), 1)
                e.wait_ge(sem("B_var"), L + 1)
                act(sqB, bank[4][:, :].rearrange("p (i s) -> p i s", i=2), ACT.Ln, bias=C("eps", 2, 3))\
                    .then_inc(sem("B_ln"), 1)
                e.wait_ge(sem("D_ktr"), L + 1)
                act(kltok, bank[2][:, 0:S].rearrange("p (t c) -> p t c", t=T), ACT.Copy).then_inc(sem("D_ktok"), 1)
                for n in range(2):
                    e.wait_ge(sem("A_ms"), 2 * L + n + 1)
                    act(sqA[:, 2 * n:2 * n + 2, :], bank[5 + n][:, :].rearrange("p (i s) -> p i s", i=2), ACT.Ln,
                        bias=C("eps", 0, 1)).then_inc(sem("A_ln"), 1)
                e.wait_ge(sem("C_ln"), L + 1)
                act(yc2, yc2, ACT.Exp, scale=-0.5).then_inc(sem("C_rs"), 1)
                e.wait_ge(sem("A_ln"), 2 * (L + 1))
                for n in range(2):
                    act(sqA[:, 2 * n:2 * n + 2, :], sqA[:, 2 * n:2 * n + 2, :], ACT.Exp, scale=-0.5)\
                        .then_inc(sem("A_rs"), 1)
                e.wait_ge(sem("B_ln"), L + 1)
                act(sqB, sqB, ACT.Exp, scale=-0.5).then_inc(sem("B_rs"), 1)
                y_high(L, 0, "y_C", L + 1)
                e.wait_ge(sem("D_ms"), L + 1)
                act(rsD, bank[2][:, :].rearrange("p (i s) -> p i s", i=2), ACT.Ln, bias=C("eps", 0, 1))\
                    .then_inc(sem("D_lnm"), 1)
                e.wait_ge(sem("D_lnm"), L + 1)
                act(rsD, rsD, ACT.Exp, scale=-0.5).then_inc(sem("D_rs"), 1)
                for t in range(T):
                    e.wait_ge(sem("A_max"), T * L + t + 1)
                    for hh in range(4):
                        s = (s0 if t == 0 else s1)[:, hh, :]
                        act(s, s, ACT.Exp, bias=negm[:, 4 * t + hh:4 * t + hh + 1],
                            accum_out=den[:, 4 * t + hh:4 * t + hh + 1]).then_inc(sem("A_exp"), 1)
                act(sgo, ogD, ACT.Silu).then_inc(sem("D_silu"), 1)
                e.wait_ge(sem("B_norm"), L + 1)
                act(yT[:, 2:4, :], acc, ACT.Silu).then_inc(sem("y_B"), 1)
                y_high(L, 1, "y_B", L + 1)
                hi(e, unit(L, 30))
                hi(e, unit(L, 31))
                y_high(L, 2, "y_D", L + 1)
                for n, b in enumerate((2, 3, 4)):
                    e.wait_ge(sem("A_tr"), 3 * L + n + 1)
                    act(pt[:, 4 * n:4 * n + 4, :], bank[b][:, :].rearrange("p (a c) -> p a c", a=4), ACT.Copy)\
                        .then_inc(sem("A_pt"), 1)
                for n in range(AHEAD):
                    hi(e, unit(L, LAYER_UNITS + n))
                for i in range(PAIRS):
                    e.wait_ge(sem("A_pv"), 2 * L + i + 1)
                    act(yT[:, i, :], bank[(7, 2)[i]][:, 0:S], ACT.Copy).then_inc(sem("y_A"), 1)
                y_high(L, 3, "y_A", 2 * L + 2)

            def silu(j, first=None, reg=None):
                wait_gate_up(e, j, first, reg)
                if j >= 2:
                    e.wait_ge(sem("hm"), at(reg, FB, j - 1))
                act(sg[:, j % 2, :], bank[j % 2][:, 0:P], ACT.Silu).then_inc(sem("silu"), 1)

            def hidden_high(j, first=None, reg=None):
                e.wait_ge(sem("ht"), at(reg, FB, j + 1))
                if j >= 2:
                    wait_down(e, j, first, reg, before=2)
                act(hthi[:, j % 2, :], bank[2][:, 0:P], ACT.Copy).then_inc(sem("hthi"), 1)

            def dense():
                norm(1)
                for b in range(FB):
                    if b > 0:
                        hi(e, DENSE_AT + 3 * b + 2)
                    if b > 0:
                        hidden_high(2 * b - 1)
                    silu(2 * b)
                    if b < FB - 1:
                        hi(e, DENSE_AT + 3 * b + 3)
                    hidden_high(2 * b)
                    if b < FB - 1:
                        hi(e, DENSE_AT + 3 * b + 4)
                    silu(2 * b + 1)
                hidden_high(2 * FB - 1)

            def x_high(reg, v):
                for k in range(2):
                    e.wait_ge(sem("M_xgf"), at(reg, 2, 2 * v + k + 1))
                    act(xhi[:, 4 * k:4 * k + 4, 0:P], xgf[:, 4 * k:4 * k + 4, :], ACT.Copy)\
                        .then_inc(sem("M_xhi"), 1)

            def experts(again, first, j0):
                for n in range(PAD if again else 0):
                    hi(e, first + n)
                v0 = (NE + 1) * again
                x_high(None, v0)
                silu(j0, first)
                with e.Fori(0, NE) as ex:
                    for b in range(FB):
                        j, u = j0 + b, first + 2 + 3 * b
                        if b > 1:
                            hi(e, u, ex)
                        if b > 0:
                            hidden_high(j - 1, first, ex)
                            hi(e, u + 1, ex)
                            silu(j, first, ex)
                            hi(e, u + 2, ex)
                        if b in (10, 14):
                            k2 = (b - 10) // 4
                            e.wait_ge(sem("M_xlo"), ex * 2 + (2 * v0 + 2))
                            e.wait_ge(sem("M_gath"), ex * 2 + (2 * v0 + 2 + k2 + 1))
                            for k in range(4):
                                ins = act(xgf[:, 4 * k2 + k, :], bank[5 + k2][:, k * P:(k + 1) * P], ACT.Copy,
                                          scale=V(1, "ffn_g", 4 * k2 + k))
                            ins.then_inc(sem("M_xgf"), 1)
                        if b == 5:
                            e.wait_ge(sem("M_selt"), ex + (NE * again + 1))
                            act(selt[:], bank[5][:, 0:S].rearrange("p (t c) -> p t c", t=T), ACT.Copy)\
                                .then_inc(sem("M_selts"), 1)
                    hidden_high(j0 + FB - 1, first, ex)
                    x_high(ex, v0 + 1)
                    hi(e, first + F_UNITS + 2, ex)
                    wait_down(e, j0 + FB - 1, first, ex)
                    for half in range(2):
                        act(y_part(xhi, half), y_psum(half), ACT.Copy).then_inc(sem("M_yhi"), 1)
                    hi(e, first + F_UNITS + 3, ex)
                    silu(j0 + FB, first + F_UNITS, ex)
                    hi(e, first + F_UNITS + 4, ex)
                    hi(e, first + F_UNITS + 5, ex)
                    e.wait_ge(sem("M_add"), ex * 4 + (4 * NE * again + 4))
                    for n in range(4):
                        e.wait_ge(sem("M_comb"), ex * 4 + (4 * NE * again + n + 1))
                        act(scaled[:, n, :], bank[COMBINE[n]][:, :], ACT.Copy, scale=gate[:, n // 2, :]).then_inc(sem("M_scaled"), 1)

            mixers(0)
            dense()
            mixers(1)
            norm(3, split=False, units=([MOE_AT + n for n in range(AHEAD, PAD)], ()))
            e.wait_ge(sem("R_dif"), 1)
            act(dif, dif, ACT.Exp).then_inc(sem("R_exp"), 1)
            experts(0, MOE_AT, 2 * FB)
            e.wait_ge(sem("R_over"), 1)
            with e.If(e.value_load(over[0:1, 0:1], min_val=0, max_val=S) > P):
                experts(1, AGAIN_AT, 2 * FB + NE * FB)

        @block.tensor
        def _(e):
            mm = e.matmul

            def norm(n):
                for j in range(4):
                    for kk in range(2):
                        for t in range(T):
                            if j == 0 and kk == 0:
                                e.wait_ge(sem("xs"), T * n + t + 1)
                            k = 2 * j + kk
                            c = (2 * kk + t) * P
                            ins = e.transpose(bank[2 + j][:, c:c + P], xs[:, t, k * P:(k + 1) * P], ident)
                    ins.then_inc(sem("xn_t"), 1)

            def three(out_, w, x_, start, stop_, w_left):
                (wh, wl), (xh, xl) = w, x_
                for n, (a, b) in enumerate(((wh, xh), (wh, xl), (wl, xh)) if w_left
                                           else ((xh, wh), (xh, wl), (xl, wh))):
                    ins = mm(out_, a, b, start=start and n == 0, stop=stop_ and n == 2, skip_group_check=True)
                return ins

            def zs_upto(L, a, b, tiles=range(T)):
                for u in range(a, b):
                    if u - 1 in V_UNITS:
                        continue
                    n = unit(L, u)
                    s, (_, rows) = n % HELD, z_at(u)
                    assert not rows or s < HELD - 1
                    e.wait_ge(sem("w_split"), n + (2 if rows else 1))
                    if u >= 2:
                        e.wait_ge(sem("z_out"), Z_UNITS * L + u - 1)
                    for t in tiles if rows else range(1):
                        for k in range(KD):
                            if u == 0 and k % 2 == 0:
                                e.wait_ge(sem("x_split"), 8 * L + k // 2 + 1)
                            c = slice(t * P, (t + 1) * P) if rows else slice(0, S)
                            w = [a_[:, s:s + 2, k * P:(k + 1) * P] if rows else a_[:, s, k * P:(k + 1) * P]
                                 for a_ in (whi, wlo)]
                            o = bank[u % 2][:, t * GROUP:(t + 1) * GROUP] if rows else bank[u % 2][:, 0:S]
                            ins = three(o, w, [a_[:, k, c] for a_ in (xhi, xlo)], k == 0, k == KD - 1, not rows)
                    if not rows or T - 1 in tiles:
                        ins.then_inc(sem("w_used"), 2 if rows else 1)

            def project(L, j):
                e.wait_ge(sem("y_split"), 4 * L + j + 1)
                if j == 0:
                    e.wait_ge(sem("z_out"), Z_UNITS * (L + 1))
                    e.wait_ge(sem("A_ln"), 2 * (L + 1))
                for i, tiles in ((0, (0, 1)), (1, (0, 1))) if j < 3 else ((0, (0,)), (1, (0,)), (0, (1,)), (1, (1,))):
                    n = unit(L, Z_UNITS + 2 * j + i)
                    e.wait_ge(sem("w_split"), n + 1)
                    s, k = n % HELD, Y_CHUNK[j] + i
                    for t in tiles:
                        for half in range(2):
                            b = PROJ[2 * t + half]
                            w = [a_[:, s, half * 512:half * 512 + 512] for a_ in (whi, wlo)]
                            ins = three(bank[b][:, :], w, [a_[:, k, t * P:(t + 1) * P] for a_ in (xhi, xlo)],
                                        j == 0 and i == 0, j == 3 and i == 1, False)
                    if T - 1 in tiles:
                        ins.then_inc(sem("w_used"), 1)
                    elif i == 1:
                        ins.then_inc(sem("y_first"), 1)

            def mixers(L):
                norm(2 * L)
                zs_upto(L, 0, 2)
                if L == 0:
                    bias()
                zs_upto(L, 2, 11)
                if L == 0:
                    e.wait_ge(sem("con2_in"), 64)
                e.wait_ge(sem("C_lin"), 3 * (L + 1))
                for q in range(3):
                    for i in range(PAIRS):
                        ins = mm(bank[2 + q][:, i * S:(i + 1) * S], lor[:, L, q, i * P:(i + 1) * P], lin,
                                 start=True, stop=True)
                ins.then_inc(sem("C_lora"), 1)
                zs_upto(L, 11, 12)
                e.wait_ge(sem("C_sq"), L + 1)
                mm(bank[5][:, :], blk, sq, start=True, stop=True).then_inc(sem("C_kk"), 1)
                zs_upto(L, 12, 13)
                e.wait_ge(sem("C_rk"), L + 1)
                mm(bank[6][:, :], blk, bonus, start=True, stop=True).then_inc(sem("C_bon"), 1)
                zs_upto(L, 13, 15)
                e.wait_ge(sem("C_g"), L + 1)
                for n, (src, ready) in enumerate(((zs[:, 4:6, :], 0), (knew, 1), (alr[:, 0], 2), (kkn, 3))):
                    e.wait_ge(sem("C_shift"), L + 1) if n == 0 else e.wait_ge(sem("C_in"), 3 * L + n)
                    for t in range(T):
                        for i in range(PAIRS):
                            ins = e.transpose(bank[2 + n][:, (2 * t + i) * P:(2 * t + i + 1) * P],
                                              src[:, i, t * P:(t + 1) * P], ident)
                    ins.then_inc(sem("C_tr"), 1)
                e.wait_ge(sem("C_rh"), L + 1)
                order = (6, 7, 2, 3, 4, 5)
                for n in range(8):
                    i, t, m = n // 4, n // 2 % 2, n % 2
                    if n == 2:
                        e.wait_ge(sem("C_tok"), 4 * (L + 1))
                    if n >= 6:
                        e.wait_ge(sem("C_mats"), 8 * L + n - 5)
                    hp, tok = slice(m * HD, (m + 1) * HD), slice(t * P, (t + 1) * P)
                    for q, src in enumerate((kkn, knew)):
                        ins = mm(bank[order[n % 6]][:, q * S:(q + 1) * S], src[hp, i, tok], alr[hp, :, i, tok],
                                 start=True, stop=True)
                    ins.then_inc(sem("C_mat"), 1)
                zs_upto(L, 15, 17)
                e.wait_ge(sem("C_mats"), 8 * (L + 1))
                for n in range(8):
                    i, t, m = n // 4, n // 2 % 2, n % 2
                    c = ((t * PAIRS + i) * 2 + m) * HD
                    ins = mm(bank[2][:, c:c + HD], mats[:, n, 2, :], vtok[:, t, i * P + m * HD:i * P + m * HD + HD],
                             start=True, stop=True)
                ins.then_inc(sem("C_bv"), 1)
                e.wait_ge(sem("z_out"), Z_UNITS * L + UD0 + 5)
                mm(bank[7][:, 0:S], g2s[:, L, :], gdD[0:16, :], start=True, stop=True).then_inc(sem("D_gk"), 1)
                e.wait_ge(sem("C_x0"), L + 1)
                for l in range(LEVELS):
                    k = LEVELS * L + l
                    for g in range(2):
                        if l > 0:
                            e.wait_ge(sem("C_x"), 2 * (k - 1) + g + 1)
                        for n in range(4 * g, 4 * g + 4):
                            o = bank[3 + g][:, (n % 4) * P:(n % 4 + 1) * P]
                            if l == 0:
                                ins = e.transpose(o, mats[:, n, 0, :], ident)
                            else:
                                ins = mm(o, mats[:, n, 0, :], X[:, n, :], start=True, stop=True)
                        ins.then_inc(sem("C_m1"), 1)
                    for g in range(2):
                        e.wait_ge(sem("C_m1s"), 2 * k + g + 1)
                        if g == 1 and l == 0:
                            e.wait_ge(sem("C_bvs"), L + 1)
                        if g == 0 and l == 0:
                            e.wait_ge(sem("D_abs"), L + 1)
                        if 0 < l < LEVELS - 1:
                            for n in range(4 * g, 4 * g + 4):
                                mm(bank[5 + g][:, (n % 4) * P:(n % 4 + 1) * P], XT[:, n, :], mats[:, n, 2, :],
                                   start=True, stop=True)
                        for n in range(4 * g, 4 * g + 4):
                            o = bank[(7, 2)[g]][:, (n % 4) * P:(n % 4 + 1) * P]
                            if l == 0:
                                ins = e.transpose(o, mats[:, n, 2, :], ident)
                            else:
                                ins = mm(o, mats[:, n, 2, :], XT[:, n, :], start=True, stop=True)
                        ins.then_inc(sem("C_p"), 1)
                    if l < LEVELS - 1:
                        zs_upto(L, 17 + l, 18 + l)
                e.wait_ge(sem("C_x"), 2 * LEVELS * (L + 1))
                for n in range(8):
                    i, t, m = n // 4, n // 2 % 2, n % 2
                    c = ((t * PAIRS + i) * 2 + m) * HD
                    ins = mm(bank[3][:, c:c + HD], XT[:, n, :], BVs[:, t, i, m, :], start=True, stop=True)
                ins.then_inc(sem("C_w"), 1)
                for n in range(8):
                    i, t, m = n // 4, n // 2 % 2, n % 2
                    ins = mm(bank[4][m * HD:(m + 1) * HD, (2 * i + t) * P:(2 * i + t + 1) * P],
                             altok[:, t, i * P + m * HD:i * P + m * HD + HD], XT[:, n, :], start=True, stop=True,
                             skip_group_check=True)
                ins.then_inc(sem("C_xa"), 1)
                e.wait_ge(sem("C_xas"), L + 1)
                for c in range(NCH):
                    t, hf = c // 2, c % 2
                    rows = slice(hf * HD, (hf + 1) * HD)
                    e.wait_ge(sem("C_st"), NCH * L + c + 1)
                    for i in range(PAIRS):
                        ins = mm(bank[5][rows, i * P:(i + 1) * P], XA[:, 2 * i + t, rows], ST[:, c, i, :],
                                 start=True, stop=True, skip_group_check=True)
                    ins.then_inc(sem("C_u"), 1)
                    if c < NCH - 1:
                        e.wait_ge(sem("C_us"), NCH * L + c + 1)
                        for i in range(PAIRS):
                            cols = slice(i * P, (i + 1) * P)
                            mm(bank[6][:, cols], betok[rows, t, cols], Us[rows, t, i, :], start=True, stop=False,
                               skip_group_check=True)
                            ins = mm(bank[6][:, cols], khtok[rows, t, cols], vtok[rows, t, cols], start=False,
                                     stop=True, skip_group_check=True)
                        ins.then_inc(sem("C_ds"), 1)
                    if c < 2:
                        zs_upto(L, 22, 24, (c,))
                e.wait_ge(sem("C_us"), NCH * (L + 1))
                e.wait_ge(sem("C_ws"), L + 1)
                for i in range(PAIRS):
                    for c in range(NCH):
                        tok = slice(c * CHUNK, (c + 1) * CHUNK)
                        mm(bank[3 + i][:, tok], ST[:, c, i, :], alr[:, 1, i, tok], start=c == 0, stop=False,
                           skip_group_check=True)
                    for t in range(T):
                        for m in range(2):
                            n = 4 * i + 2 * t + m
                            o = bank[3 + i][m * HD:(m + 1) * HD, t * P:(t + 1) * P]
                            mm(o, Us[:, t, i, m * HD:(m + 1) * HD], mats[:, n, 1, :], start=False, stop=False,
                               skip_group_check=True)
                            ins = mm(o, vtok[:, t, i * P + m * HD:i * P + (m + 1) * HD], mats[:, n, 3, :],
                                     start=False, stop=True, skip_group_check=True)
                    ins.then_inc(sem("C_o"), 1)
                e.wait_ge(sem("D_qx"), L + 1)
                for t in range(T):
                    mm(bank[(2, 7)[t]][:, :], kd[:, t * P:(t + 1) * P], qx[:, :, t * P:(t + 1) * P],
                       start=True, stop=True).then_inc(sem("D_att"), 1)
                e.wait_ge(sem("C_oc"), L + 1)
                mm(bank[5][:, :], blk, yC, start=True, stop=True).then_inc(sem("C_mean"), 1)
                e.wait_ge(sem("B_acc"), L + 1)
                mm(bank[3][:, :], blk, acc, start=True, stop=True).then_inc(sem("B_mean"), 1)
                e.wait_ge(sem("D_atts"), T * L + 1)
                for t in range(T):
                    ins = e.transpose(bank[2][:, t * P:(t + 1) * P], kl[:, t * P:(t + 1) * P], ident)
                ins.then_inc(sem("D_ktr"), 1)
                e.wait_ge(sem("C_xc"), L + 1)
                mm(bank[6][:, :], blk, yc2, start=True, stop=True).then_inc(sem("C_var"), 1)
                e.wait_ge(sem("B_xc"), L + 1)
                mm(bank[4][:, :], blk, sqB, start=True, stop=True).then_inc(sem("B_var"), 1)
                for n in range(2):
                    e.wait_ge(sem("A_sq"), 2 * L + n + 1)
                    if n == 1:
                        e.wait_ge(sem("C_ln"), L + 1)
                    mm(bank[5 + n][:, :], blk, sqA[:, 2 * n:2 * n + 2, :], start=True, stop=True)\
                        .then_inc(sem("A_ms"), 1)
                e.wait_ge(sem("D_ktok"), L + 1)
                e.wait_ge(sem("D_atts"), T * (L + 1))
                for c in range(NCH - 1):
                    rows = slice((c % 2) * HD, (c % 2 + 1) * HD)
                    mm(con_D(c), kltok[rows, c // 2, :], vD[rows, c // 2, :], start=True, stop=True,
                       skip_group_check=True).then_inc(sem("D_con"), 1)
                e.wait_ge(sem("B_ln"), L + 1)
                for i in range(PAIRS):
                    for t in range(T):
                        for m in range(2):
                            hh = 2 * i + m
                            mm(bank[3 + i][m * HD:(m + 1) * HD, t * P:(t + 1) * P], vD[:, t, hh * HD:(hh + 1) * HD],
                               attD[:, t, hh, :], start=t == 0, stop=False, skip_group_check=True)
                    for c in range(1, NCH):
                        e.wait_ge(sem("D_st"), (NCH - 1) * L + c)
                        tok = slice(c * CHUNK, (c + 1) * CHUNK)
                        ins = mm(bank[3 + i][:, tok], SD[:, c, i * P:(i + 1) * P], qd[:, tok], start=False,
                                 stop=c == NCH - 1, skip_group_check=True)
                    ins.then_inc(sem("D_o"), 1)
                e.wait_ge(sem("D_sq"), L + 1)
                mm(bank[2][:, :], blk, sqD, start=True, stop=True).then_inc(sem("D_ms"), 1)
                e.wait_ge(sem("A_qk"), L + 1)
                for n, b in enumerate((7, 3, 4, 2)):
                    t, i = n // 2, n % 2
                    kj = P * (t + 1)
                    if n == 3:
                        e.wait_ge(sem("D_lnm"), L + 1)
                    mm(bank[b][:, 0:2 * kj], qn[:, i, t * P:(t + 1) * P], kx[:, :, i, 0:kj], start=True, stop=True)\
                        .then_inc(sem("A_s"), 1)
                project(L, 0)
                for n, b in enumerate((2, 3, 4)):
                    e.wait_ge(sem("A_p"), T * (L + 1))
                    for q in range(4):
                        if n == 0:
                            src = s0[:, q, :]
                        else:
                            src = s1[:, 2 * (n - 1) + q // 2, (q % 2) * P:(q % 2 + 1) * P]
                        ins = e.transpose(bank[b][:, q * P:(q + 1) * P], src, ident)
                    ins.then_inc(sem("A_tr"), 1)
                project(L, 1)
                e.wait_ge(sem("A_pt"), 3 * (L + 1))
                for i in range(PAIRS):
                    for m in range(2):
                        hh = 2 * i + m
                        o = bank[(7, 2)[i]][m * HD:(m + 1) * HD, :]
                        vv = [vA[:, jt, hh * HD:(hh + 1) * HD] for jt in range(T)]
                        mm(o[:, 0:P], vv[0], pt[:, hh, :], start=True, stop=False, skip_group_check=True)
                        mm(o[:, P:S], vv[0], pt[:, 4 + 2 * hh, :], start=False, stop=False, skip_group_check=True)
                        ins = mm(o[:, P:S], vv[1], pt[:, 5 + 2 * hh, :], start=False, stop=True,
                                 skip_group_check=True)
                    ins.then_inc(sem("A_pv"), 1)
                project(L, 2)
                project(L, 3)

            def bias():
                e.wait_ge(sem("ext_in"), 32)
                for hh in range(4):
                    ins = mm(bank[2 + hh][:, 0:3 * P], rel[:, hh, :], bkt[0:32, :], start=True, stop=True)
                ins.then_inc(sem("ext_mm"), 1)

            e.wait_ge(sem("con_in"), 32)

            def gate_up(j, part, unit_, tok, reg=None):
                e.wait_ge(sem("w_split"), at(reg, F_UNITS, unit_ + 1))
                if part == 0 and j >= 2:
                    e.wait_ge(sem("hm"), at(reg, FB, j - 1))
                s = unit_ % HELD
                for k in range(4):
                    w = [a_[:, s, k * 256:(k + 1) * 256] for a_ in (whi, wlo)]
                    ins = three(bank[j % 2][:, 0:256], w, [a_[:, 4 * part + k, tok] for a_ in (xhi, xlo)],
                                part == 0 and k == 0, part == 1 and k == 3, False)
                return ins

            def turn(j, reg=None):
                e.wait_ge(sem("hm"), at(reg, FB, j + 1))
                e.transpose(bank[2][:, 0:P], hm[:, j % 2, :], ident).then_inc(sem("ht"), 1)

            def down(j, unit_, banks, start, stop_, reg=None):
                e.wait_ge(sem("htlo"), at(reg, FB, j + 1))
                e.wait_ge(sem("w_split"), at(reg, F_UNITS, unit_ + 1))
                s = unit_ % HELD
                for half in range(2):
                    w = [a_[:, s, half * 512:half * 512 + 512] for a_ in (whi, wlo)]
                    ins = three(bank[banks[half]][:, :], w, [a_[:, j % 2, :] for a_ in (hthi, htlo)],
                                start, stop_, False)
                return ins

            def dense():
                norm(1)
                for j in range(2 * FB + 1):
                    b, t = j // 2, j % 2
                    n = DENSE_AT + 3 * b
                    tok = slice(t * P, (t + 1) * P)
                    pb_, pt_ = (j - 1) // 2, (j - 1) % 2
                    if j < 2 * FB:
                        if j == 0:
                            e.wait_ge(sem("x_split"), 6)
                        ins = gate_up(j, 0, n, tok)
                        if t == 1:
                            ins.then_inc(sem("w_used"), 1)
                    if j > 0:
                        turn(j - 1)
                    if j < 2 * FB:
                        if j == 0:
                            e.wait_ge(sem("x_split"), 8)
                        gate_up(j, 1, n + 1, tok).then_inc(sem("w_used" if t == 1 else "gu"), 1)
                    if j > 0:
                        ins = down(j - 1, DENSE_AT + 3 * pb_ + 2, (3 + 2 * pt_, 4 + 2 * pt_), pb_ == 0,
                                   pb_ == FB - 1)
                        ins.then_inc(sem("w_used" if pt_ == 1 else "down"), 1)

            def gather_half(k2, reg, v):
                e.wait_ge(sem("M_sel"), at(reg, 1, v + 1))
                for k in range(4):
                    for t in range(T):
                        kk = 4 * k2 + k
                        ins = mm(bank[5 + k2][:, k * P:(k + 1) * P], xs[:, t, kk * P:(kk + 1) * P], sel[:, t, :],
                                 start=t == 0, stop=t == 1, skip_group_check=True)
                ins.then_inc(sem("M_gath"), 1)

            def experts(again, first, j0):
                v0 = (NE + 1) * again
                if again:
                    e.wait_ge(sem("M_scaled"), 4 * NE)
                    e.wait_ge(sem("M_sel"), v0 + 1)
                    e.transpose(bank[5][:, 0:P], sel[:, 0, :], ident).then_inc(sem("w_used"), PAD - 2)
                gather_half(0, None, v0)
                gather_half(1, None, v0)
                tok = slice(0, P)
                for k in range(2):
                    e.wait_ge(sem("M_xlo"), 2 * v0 + k + 1)
                for part in range(2):
                    gate_up(j0, part, first + part, tok).then_inc(sem("w_used"), 1)
                with e.Fori(0, NE) as ex:
                    for b in range(1, FB + 1):
                        j = j0 + b
                        if b < FB:
                            u = first + gu_unit(b)
                            gate_up(j, 0, u, tok, ex).then_inc(sem("w_used"), 1)
                        turn(j - 1, ex)
                        if b < FB:
                            gate_up(j, 1, u + 1, tok, ex).then_inc(sem("w_used"), 1)
                        down(j - 1, first + wd_unit(b - 1), (3, 4), b == 1, b == FB, ex).then_inc(sem("w_used"), 1)
                        if b == 4:
                            for t in range(T):
                                ins = e.transpose(bank[5][:, t * P:(t + 1) * P], sel[:, t, :], ident)
                            ins.then_inc(sem("M_selt"), 1)
                        if b == 8:
                            e.wait_ge(sem("M_selts"), ex + (NE * again + 1))
                            gather_half(0, ex, v0 + 1)
                        if b == 12:
                            gather_half(1, ex, v0 + 1)
                    for part in range(2):
                        e.wait_ge(sem("M_xlo"), ex * 2 + (2 * v0 + 2 + part + 1))
                        gate_up(j0 + FB, part, first + F_UNITS + part, tok, ex).then_inc(sem("w_used"), 1)
                    for n in range(4):
                        t, half = n // 2, n % 2
                        if n < 2:
                            e.wait_ge(sem("M_ylo"), ex * 2 + (2 * NE * again + n + 1))
                        for q, part in enumerate((xhi, xlo)):
                            ins = mm(bank[COMBINE[n]][:, :], selt[:, t, :], y_part(part, half),
                                     start=q == 0, stop=q == 1)
                        ins.then_inc(sem("M_comb"), 1)

            mixers(0)
            dense()
            mixers(1)
            norm(3)
            for k in range(KD):
                e.wait_ge(sem("xnf"), 12 + k // 2 + 1)
                for t in range(T):
                    ins = mm(bank[6 + t][:, 0:NE], xnf[:, k, t * P:(t + 1) * P], rou[:, k, :],
                             start=k == 0, stop=k == KD - 1)
                    if k == KD - 1:
                        ins.then_inc(sem("R_lg"), 1)
            e.wait_ge(sem("R_mk"), 1)
            mm(bank[2][:, 0:8], C("upper"), mk[:, 0, :], start=True, stop=True)
            mm(bank[2][:, 8:16], C("upper"), mk[:, 1, :], start=True, stop=False)
            mm(bank[2][:, 8:16], C("ones"), mk[:, 0, :], start=False, stop=True)
            mm(bank[2][:, 16:24], C("ones"), mk[:, 0, :], start=True, stop=False)
            mm(bank[2][:, 16:24], C("ones"), mk[:, 1, :], start=False, stop=True).then_inc(sem("R_rank"), 1)
            experts(0, MOE_AT, 2 * FB)
            e.wait_ge(sem("R_over"), 1)
            with e.If(e.value_load(over[0:1, 0:1], min_val=0, max_val=S) > P):
                experts(1, AGAIN_AT, 2 * FB + NE * FB)

        @block.gpsimd
        def _(e):
            ch = Chain(e, sem("pool_chain"))

            def conv(L):
                e.wait_ge(sem("z_out"), Z_UNITS * L + UD0)
                e.memset(hB[:, :, 0:CW - 1], 0.0)
                e.wait_ge(sem("B_sig"), L + 1)
                ch(e.tensor_tensor(hB[:, :, CW - 1:], uB, gB, ALU.mult))
                bias_ = V(L, "conv_b", 0, 2).unsqueeze(2).to_broadcast([P, PAIRS, S])
                for j in range(CW):
                    w = V(L, "conv_w", 2 * j, 2).unsqueeze(2).to_broadcast([P, PAIRS, S])
                    ch(e.tensor_tensor(tap[:], hB[:, :, j:j + S], w, ALU.mult))
                    ins = e.tensor_tensor(acc, tap[:], acc if j > 0 else bias_, ALU.add)
                    if j < CW - 1:
                        ch(ins)
                ins.then_inc(sem("B_acc"), 1)
                e.wait_ge(sem("C_o"), 2 * (L + 1))
                for n in range(2):
                    e.tensor_tensor(sqA[:, 2 * n:2 * n + 2, :], qkA[:, 2 * n:2 * n + 2, :],
                                    qkA[:, 2 * n:2 * n + 2, :], ALU.mult).then_inc(sem("A_sq"), 1)

            e.wait_ge(sem("ext_sb"), 4)
            e.dma_start(ext_dram, ext).then_inc(sem("ext_out"), 16)
            e.wait_ge(sem("ext_out"), 16)
            for t, dst in ((0, bias0), (1, bias1)):
                src = bass.AP(ext_dram.tensor, S - 1 - P * t, [[4 * 3 * P - 1, P], [3 * P, 4], [1, P * (t + 1)]])
                e.dma_start(dst[:], src).then_inc(sem("bias_in"), 16)
            e.wait_ge(sem("con_in"), 32)
            conv(0)
            conv(1)

            def experts(again):
                v = (NE + 1) * again + 1
                with e.Fori(0, NE) as ex:
                    e.wait_ge(sem("M_xlo"), ex * 2 + (2 * v + 1))
                    rows_low(e, 1, ex, v)
                    for n in range(4):
                        t, c = n // 2, slice((n % 2) * 512, (n % 2 + 1) * 512)
                        e.wait_ge(sem("M_scaled"), ex * 4 + (4 * NE * again + n + 1))
                        e.tensor_tensor(h[:, t, c], h[:, t, c], scaled[:, n, :], ALU.add).then_inc(sem("M_add"), 1)
                e.wait_ge(sem("M_add"), 4 * NE * (again + 1) + 4)
                e.memset(small[:, 62:63], 0.0).then_inc(sem("h_done"), 1)

            e.memset(small[:, 61:62], 0.0).then_inc(sem("M_add"), 4)
            experts(0)
            e.wait_ge(sem("R_over"), 1)
            with e.If(e.value_load(over[0:1, 0:1], min_val=0, max_val=S) > P):
                experts(1)

        @block.vector
        def _(e):
            ch = Chain(e, sem("dve_chain"))
            tt, ts, stt = e.tensor_tensor, e.tensor_scalar, e.scalar_tensor_tensor

            def norm(n, split=True, units=()):
                e.wait_ge(sem("rms"), n + 1)
                ch(e.reciprocal(rstd, rstd))
                for t in range(T):
                    ts(xs[:, t, :], h[:, t, :], rstd[:, t:t + 1], None, ALU.mult).then_inc(sem("xs"), 1)
                for u in units:
                    lo(e, u)
                g = V(n // 2, "mix_g" if n % 2 == 0 else "ffn_g", 0, KD)

                def x_low(j):
                    e.wait_ge(sem("xnf"), 4 * n + j + 1)
                    e.wait_ge(sem("xhi"), 4 * n + j + 1)
                    tt(xlo[:, 2 * j:2 * j + 2, :], xnf[:, 2 * j:2 * j + 2, :],
                       xhi[:, 2 * j:2 * j + 2, :].bitcast(F32), ALU.subtract).then_inc(sem("x_split"), 1)

                for j in range(4):
                    e.wait_ge(sem("xn_t"), 4 * n + j + 1)
                    tt(xnf[:, 2 * j:2 * j + 2, :], bank[2 + j][:, :].rearrange("p (k s) -> p k s", k=2),
                       g[:, 2 * j:2 * j + 2].unsqueeze(2).to_broadcast([P, 2, S]), ALU.mult)\
                        .then_inc(sem("xnf"), 1)
                    if split and j > 0:
                        x_low(j - 1)
                if split:
                    x_low(3)

            def los(L, a, b):
                for u in range(a, b):
                    lo(e, unit(L, u))

            def y_low(L, j, name, n):
                e.wait_ge(sem("yhi"), 4 * L + j + 1)
                e.wait_ge(sem(name), n)
                k = Y_CHUNK[j]
                tt(xlo[:, k:k + 2, :], yT[:, k:k + 2, :], xhi[:, k:k + 2, :].bitcast(F32), ALU.subtract)\
                    .then_inc(sem("y_split"), 1)

            def mixers(L):
                if L > 0:
                    los(L, 0, 1)
                norm(2 * L, units=(unit(L, L),))
                e.memset(zC[:, :, 0:1], 0.0).then_inc(sem("C_zero"), 1)
                los(L, L + 1, HELD + 7)
                if L == 0:
                    e.wait_ge(sem("con2_in"), 64)
                e.wait_ge(sem("z_out"), Z_UNITS * L + 7)
                e.wait_ge(sem("C_zero"), L + 1)
                ch(tt(zs, zC[:, :, 0:S], zC[:, :, 1:S + 1], ALU.subtract))
                for u in (6, 4, 5, 2, 3, 0, 1):
                    ins = stt(zs[:, u, :], zs[:, u, :], V(L, "mu", u), zC[:, u, 1:S + 1], ALU.mult, ALU.add)
                ins.then_inc(sem("C_shift"), 1)
                e.wait_ge(sem("C_shift"), L + 1)
                for i in range(PAIRS):
                    ins = ts(kkn[:, i, :], zs[:, 2 + i, :], V(L, "k_k", i), None, ALU.mult)
                ch(ins)
                tt(sq, kkn, kkn, ALU.mult).then_inc(sem("C_sq"), 1)
                for m in (X, XT):
                    for g in range(2):
                        ins = e.tensor_copy(m[:, 4 * g:4 * g + 4, :], over4(ident))
                ins.then_inc(sem("C_x0"), 1)
                e.wait_ge(sem("C_sga"), 2 * (L + 1))
                for i in range(PAIRS):
                    ins = ts(knew[:, i, :], sga[:, i, :], 1.0, V(L, "k_a", i), ALU.subtract, ALU.mult)
                ch(ins)
                ch(stt(knew, knew, 1.0, zs[:, 2:4, :], ALU.add, ALU.mult))
                for i in range(PAIRS):
                    ins = stt(bonus[:, i, :], zs[:, i, :], V(L, "r_k", i), knew[:, i, :], ALU.mult, ALU.mult)
                ins.then_inc(sem("C_rk"), 1)
                los(L, HELD + 7, HELD + 9)
                e.wait_ge(sem("C_sgw"), 2 * (L + 1))
                for i in range(PAIRS):
                    ins = e.tensor_tensor_scan(cum[:, i, :], C("restart"), sgw[:, i, :], 0.0, ALU.mult, ALU.add)
                ch(ins)
                tt(sgw, cum, sgw, ALU.subtract).then_inc(sem("C_cum"), 1)
                e.wait_ge(sem("C_kk"), L + 1)
                ts(sq, bank[5][:, :].rearrange("p (i s) -> p i s", i=2), 1e-24 / HD, None, ALU.max)\
                    .then_inc(sem("C_kmax"), 1)
                e.wait_ge(sem("C_kn"), L + 1)
                ch(tt(kkn, sq, kkn, ALU.mult))
                ch(tt(sga, kkn, sga, ALU.mult))
                e.wait_ge(sem("C_bon"), L + 1)
                stt(bonus, bank[6][:, :].rearrange("p (i s) -> p i s", i=2), float(HD), zs[:, 4:6, :],
                    ALU.mult, ALU.mult).then_inc(sem("C_bonus"), 1)
                e.wait_ge(sem("C_exp"), 3 * L + 1)
                tt(knew, knew, cinv, ALU.mult).then_inc(sem("C_in"), 1)
                e.wait_ge(sem("C_exp"), 3 * L + 2)
                stt(alr[:, 0], kkn, -1.0, sgw, ALU.mult, ALU.mult).then_inc(sem("C_in"), 1)
                e.wait_ge(sem("C_in"), 3 * L + 2)
                tt(kkn, sga, cinv, ALU.mult).then_inc(sem("C_in"), 1)
                e.wait_ge(sem("C_exp"), 3 * L + 3)
                ch(e.tensor_copy(cend, alr[:, 1].rearrange("p i (c s) -> p i c s", s=CHUNK)[:, :, :, CHUNK - 1]))
                tt(alr[:, 1], alr[:, 1], zs[:, 0:2, :], ALU.mult).then_inc(sem("C_rh"), 1)
                los(L, HELD + 9, HELD + 10)
                e.wait_ge(sem("C_in"), 3 * (L + 1))
                e.memset(ST, 0.0).then_inc(sem("C_st"), 1)
                if L == 0:
                    e.wait_ge(sem("ext_out"), 16)
                order = (6, 7, 2, 3, 4, 5)
                for n in range(8):
                    e.wait_ge(sem("C_mat"), 8 * L + n + 1)
                    tt(mats[:, n, :, :], bank[order[n % 6]][:, :].rearrange("p (a c) -> p a c", a=4),
                       C("mask_g").rearrange("p (a c) -> p a c", a=4), ALU.mult).then_inc(sem("C_mats"), 1)
                los(L, HELD + 10, HELD + 13)
                e.wait_ge(sem("D_gk"), L + 1)
                ch(ts(cumd, bank[7][:, 0:S], V(L, "gb"), None, ALU.add))
                stt(els, cumd, -1.0, cumd, ALU.mult, ALU.min).then_inc(sem("D_abs"), 1)
                e.wait_ge(sem("C_bv"), L + 1)
                e.wait_ge(sem("C_x0"), L + 1)
                for l in range(LEVELS):
                    k = LEVELS * L + l
                    for g in range(2):
                        e.wait_ge(sem("C_m1"), 2 * k + g + 1)
                        tt(mats[:, 4 * g:4 * g + 4, 2, :], bank[3 + g][:, :].rearrange("p (a c) -> p a c", a=4),
                           over4(C("lvl", l * P, (l + 1) * P)), ALU.mult).then_inc(sem("C_m1s"), 1)
                    for g in range(2):
                        e.wait_ge(sem("C_p"), 2 * k + g + 1)
                        four = slice(4 * g, 4 * g + 4)
                        if l == 0:
                            e.wait_ge(sem("C_m1s"), 2 * k + g + 1)
                            tt(X[:, four, :], X[:, four, :], mats[:, four, 2, :], ALU.add)
                        elif l < LEVELS - 1:
                            tt(X[:, four, :], X[:, four, :], bank[5 + g][:, :].rearrange("p (a c) -> p a c", a=4),
                               ALU.add)
                        tt(XT[:, four, :], XT[:, four, :],
                           bank[(7, 2)[g]][:, :].rearrange("p (a c) -> p a c", a=4), ALU.add)\
                            .then_inc(sem("C_x"), 1)
                    if l == 0:
                        e.wait_ge(sem("D_ln"), L + 1)
                        ch(stt(lsg, cumd, 0.0, els, ALU.min, ALU.subtract))
                        ch(e.tensor_tensor_scan(cumd, C("restart"), lsg, 0.0, ALU.mult, ALU.add))
                        c4 = cumd.rearrange("p (c s) -> p c s", s=CHUNK)
                        tt(dl.rearrange("p (c s) -> p c s", s=CHUNK),
                           c4[:, :, CHUNK - 1:CHUNK].to_broadcast([P, NCH, CHUNK]), c4, ALU.subtract)\
                            .then_inc(sem("D_cum"), 1)
                    elif l == 1:
                        e.wait_ge(sem("D_exp"), 3 * (L + 1))
                        ch(stt(qd, qkD[:, 0, :], 32 ** -0.5, eb, ALU.mult, ALU.mult))
                        tt(kd, qkD[:, 1, :], enb, ALU.mult)
                        tt(kl, qkD[:, 1, :], dl, ALU.mult)
                    elif l == 2:
                        for q in range(4):
                            ins = ts(qx[:, q, :], qd, C("head32", q, q + 1), None, ALU.mult)
                        ins.then_inc(sem("D_qx"), 1)
                    los(L, HELD + 13 + l, HELD + 14 + l)
                e.wait_ge(sem("C_ws"), L + 1)
                for c in range(NCH):
                    t, rows = c // 2, slice((c % 2) * HD, (c % 2 + 1) * HD)
                    if c < NCH - 1:
                        e.wait_ge(sem("C_st"), NCH * L + c + 1)
                        for i in range(PAIRS):
                            ins = ts(stc[:, i, :], ST[:, c, i, :], cend[:, i, c:c + 1], None, ALU.mult)
                        ch(ins)
                    e.wait_ge(sem("C_u"), NCH * L + c + 1)
                    tt(Us[rows, t, :, :], bank[5][rows, 0:S].rearrange("p (i v) -> p i v", i=PAIRS),
                       Ws[rows, t, :, :], ALU.add).then_inc(sem("C_us"), 1)
                    if c < NCH - 1:
                        e.wait_ge(sem("C_ds"), (NCH - 1) * L + c + 1)
                        for i in range(PAIRS):
                            for m in range(2):
                                d = slice(m * HD, (m + 1) * HD)
                                ins = stt(ST[d, c + 1, i, d], bank[6][d, i * P + m * HD:i * P + (m + 1) * HD],
                                          cend[d, i, c:c + 1], stc[d, i, d], ALU.mult, ALU.add)
                        ins.then_inc(sem("C_st"), 1)
                    los(L, HELD + 19 + c, HELD + 20 + c)
                for i in range(PAIRS):
                    e.wait_ge(sem("C_o"), 2 * L + i + 1)
                    ins = e.tensor_copy(yC[:, i, :], bank[3 + i][:, 0:S])
                ins.then_inc(sem("C_oc"), 1)
                for t in range(T):
                    e.wait_ge(sem("D_att"), T * L + t + 1)
                    tt(attD[:, t, :, :], bank[(2, 7)[t]][:, :].rearrange("p (a c) -> p a c", a=4),
                       over4(C("mask_g", P, 2 * P)), ALU.mult).then_inc(sem("D_atts"), 1)
                e.wait_ge(sem("C_oc"), L + 1)
                e.wait_ge(sem("C_mean"), L + 1)
                ch(tt(yC, yC, bank[5][:, :].rearrange("p (i s) -> p i s", i=2), ALU.subtract))
                tt(yc2, yC, yC, ALU.mult).then_inc(sem("C_xc"), 1)
                e.wait_ge(sem("B_mean"), L + 1)
                ch(tt(acc, acc, bank[3][:, :].rearrange("p (i s) -> p i s", i=2), ALU.subtract))
                tt(sqB, acc, acc, ALU.mult).then_inc(sem("B_xc"), 1)
                los(L, HELD + 23, HELD + 24)
                e.wait_ge(sem("D_con"), (NCH - 1) * (L + 1))
                for c in range(NCH - 1):
                    if c == 0:
                        tt(SD[:, 1, :], con_D(0), C("bd_d"), ALU.mult).then_inc(sem("D_st"), 1)
                    else:
                        e.wait_ge(sem("D_st"), (NCH - 1) * L + c)
                        ch(tt(cm, con_D(c), C("bd_d"), ALU.mult))
                        stt(SD[:, c + 1, :], SD[:, c, :], eb[:, c * CHUNK + CHUNK - 1:(c + 1) * CHUNK], cm,
                            ALU.mult, ALU.add).then_inc(sem("D_st"), 1)
                e.wait_ge(sem("C_rs"), L + 1)
                ch(tt(yC, yC, yc2, ALU.mult))
                for i in range(PAIRS):
                    ins = ts(yC[:, i, :], yC[:, i, :], V(L, "ln_g", i), V(L, "ln_b", i), ALU.mult, ALU.add)
                ch(ins)
                ch(tt(yC, yC, bonus, ALU.add))
                tt(yT[:, 4:6, :], yC, gC, ALU.mult).then_inc(sem("y_C"), 1)
                e.wait_ge(sem("A_rs"), 2 * (L + 1))
                stt(qn, qkA[:, 0:2, :], V(L, "q_g"), sqA[:, 0:2, :], ALU.mult, ALU.mult)
                for m in range(2):
                    ins = stt(kx[:, m], qkA[:, 2:4, :], V(L, f"k_g{m}"), sqA[:, 2:4, :], ALU.mult, ALU.mult)
                ins.then_inc(sem("A_qk"), 1)
                for i in range(PAIRS):
                    e.wait_ge(sem("D_o"), 2 * L + i + 1)
                    ins = e.tensor_copy(oD[:, i, :], bank[3 + i][:, 0:S])
                ch(ins)
                tt(sqD, oD, oD, ALU.mult).then_inc(sem("D_sq"), 1)
                y_low(L, 0, "y_C", L + 1)
                e.wait_ge(sem("B_rs"), L + 1)
                ch(tt(acc, acc, sqB, ALU.mult))
                for i in range(PAIRS):
                    ins = ts(acc[:, i, :], acc[:, i, :], V(L, "conv_g", i), V(L, "conv_lb", i), ALU.mult, ALU.add)
                ins.then_inc(sem("B_norm"), 1)
                if L == 0:
                    e.wait_ge(sem("bias_in"), 32)
                    lm = C("logm")
                    tt(bias0[:], bias0[:], over4(lm[:, 0:P]), ALU.add)
                    ch(tt(bias1[:], bias1[:], lm[:, P:3 * P].unsqueeze(1).to_broadcast([P, 4, S]), ALU.add))
                for n, b in enumerate((7, 3, 4, 2)):
                    t, i = n // 2, n % 2
                    kj = P * (t + 1)
                    e.wait_ge(sem("A_s"), 4 * L + n + 1)
                    s, bi = ((s0, bias0), (s1, bias1))[t]
                    ins = stt(s[:, 2 * i:2 * i + 2, :], bank[b][:, 0:2 * kj].rearrange("p (m j) -> p m j", m=2),
                              1.0 / math.sqrt(HD), bi[:, 2 * i:2 * i + 2, :], ALU.mult, ALU.add)
                    if i == 1:
                        ch(ins)
                        mx = negm[:, 4 * t:4 * t + 4]
                        ch(e.tensor_reduce(mx, s, AX_X, ALU.max))
                        ts(mx, mx, -1.0, None, ALU.mult).then_inc(sem("A_max"), 1)
                e.wait_ge(sem("D_rs"), L + 1)
                ch(stt(oD, oD, V(L, "gn_g"), rsD, ALU.mult, ALU.mult))
                for t in range(T):
                    e.wait_ge(sem("A_exp"), 8 * L + 4 * t + 4)
                    s = (s0, s1)[t]
                    r4 = rden[:, 4 * t:4 * t + 4]
                    ch(e.reciprocal(r4, den[:, 4 * t:4 * t + 4]))
                    tt(s, s, r4.unsqueeze(2).to_broadcast([P, 4, P * (t + 1)]), ALU.mult).then_inc(sem("A_p"), 1)
                y_low(L, 1, "y_B", L + 1)
                e.wait_ge(sem("D_silu"), L + 1)
                tt(yT[:, 6:8, :], oD, sgo, ALU.mult).then_inc(sem("y_D"), 1)
                y_low(L, 2, "y_D", L + 1)
                los(L, 30, LAYER_UNITS + AHEAD)
                y_low(L, 3, "y_A", 2 * L + 2)
                for t in range(T):
                    e.wait_ge(sem("y_first"), L + 1) if t == 0 else e.wait_ge(sem("w_used"), unit(L, LAYER_UNITS))
                    for half in range(2):
                        c = slice(half * 512, half * 512 + 512)
                        ins = tt(h[:, t, c], h[:, t, c], bank[PROJ[2 * t + half]][:, :], ALU.add)
                    ins.then_inc(sem("h_first" if t == 0 else "h_done"), 1)
                e.wait_ge(sem("h_done"), 2 * L + 1)

            def hidden(j, reg=None, extra=0):
                e.wait_ge(sem("silu"), at(reg, FB, j + 1 + extra))
                if j >= 2:
                    e.wait_ge(sem("ht"), at(reg, FB, j - 1))
                tt(hm[:, j % 2, :], sg[:, j % 2, :], bank[j % 2][:, P:2 * P], ALU.mult).then_inc(sem("hm"), 1)

            def hidden_low(j, reg=None):
                e.wait_ge(sem("hthi"), at(reg, FB, j + 1))
                tt(htlo[:, j % 2, :], bank[2][:, 0:P], hthi[:, j % 2, :].bitcast(F32), ALU.subtract)\
                    .then_inc(sem("htlo"), 1)

            def dense():
                norm(1)
                for b in range(FB):
                    if b > 0:
                        lo(e, DENSE_AT + 3 * b + 2)
                    if b > 0:
                        hidden_low(2 * b - 1)
                    hidden(2 * b)
                    if b < FB - 1:
                        lo(e, DENSE_AT + 3 * b + 3)
                    hidden_low(2 * b)
                    if b < FB - 1:
                        lo(e, DENSE_AT + 3 * b + 4)
                    hidden(2 * b + 1)
                hidden_low(2 * FB - 1)
                for t in range(T):
                    wait_down(e, 2 * FB - 2 + t)
                    for half in range(2):
                        c = slice(half * 512, half * 512 + 512)
                        ins = tt(h[:, t, c], h[:, t, c], bank[3 + 2 * t + half][:, :], ALU.add)
                    ins.then_inc(sem("h_first" if t == 0 else "h_done"), 1)
                e.wait_ge(sem("h_done"), 2)

            def experts(again, first, j0):
                slots = C("iota", P * again, P * again + P)
                v0 = (NE + 1) * again
                if again:
                    e.wait_ge(sem("M_gath"), 2 * v0)
                choose(e, slots, None, 0).then_inc(sem("M_sel"), 1)
                for n in range(PAD if again else 0):
                    lo(e, first + n)
                if again:
                    e.wait_ge(sem("M_xlo"), 2 * v0)
                rows_of(e, 0, None, v0)
                rows_of(e, 1, None, v0)
                e.wait_ge(sem("M_xgf"), 2 * v0 + 2)
                rows_low(e, 0, None, v0)
                rows_low(e, 1, None, v0)
                with e.Fori(0, NE) as ex:
                    for b in range(FB):
                        j, u = j0 + b, first + 2 + 3 * b
                        if b > 1:
                            lo(e, u, ex)
                        if b > 0:
                            hidden_low(j - 1, ex)
                            lo(e, u + 1, ex)
                        hidden(j, ex, again)
                        if 0 < b < FB - 1:
                            lo(e, u + 2, ex)
                        if b == 3:
                            for t in range(T):
                                ts(gate[:, t, :], C("ones", 0, 1), gat[:, t, bass.ds(ex, 1)], None, ALU.mult)
                        if b == 6:
                            e.wait_ge(sem("M_gath"), ex * 2 + (2 * v0 + 2))
                            e.wait_ge(sem("M_selt"), ex + (NE * again + 1))
                            choose(e, slots, ex, 1).then_inc(sem("M_sel"), 1)
                    hidden_low(j0 + FB - 1, ex)
                    rows_low(e, 0, ex, v0 + 1)
                    lo(e, first + F_UNITS + 1, ex)
                    for half in range(2):
                        e.wait_ge(sem("M_yhi"), ex * 2 + (2 * NE * again + half + 1))
                        tt(y_part(xlo, half), y_psum(half), y_part(xhi, half).bitcast(F32), ALU.subtract)\
                            .then_inc(sem("M_ylo"), 1)
                    lo(e, first + F_UNITS + 2, ex)
                    lo(e, first + F_UNITS + 3, ex)
                    lo(e, first + F_UNITS + 4, ex)
                    lo(e, first + F_UNITS + 5, ex)

            def route():
                for t in range(T):
                    e.wait_ge(sem("R_lg"), t + 1)
                    ins = e.tensor_copy(lg[:, t, :], bank[6 + t][:, 0:NE])
                ch(ins)
                for t in range(T):
                    ins = e.max(top[:, t, :], lg[:, t, :])
                ch(ins)
                for t in range(T):
                    ins = e.max_index(idx[:, t, :], top[:, t, :], lg[:, t, :])
                ch(ins)
                ch(e.tensor_copy(idxf, idx[:]))
                for t in range(T):
                    for q, dst in enumerate((e1, e2)):
                        ins = ts(dst[:, t, :], C("iota8"), idxf[:, t, q:q + 1], None, ALU.is_equal)
                ch(ins)
                tt(mk, e1, e2, ALU.add).then_inc(sem("R_mk"), 1)
                tt(dif, top[:, :, 1:2], top[:, :, 0:1], ALU.subtract).then_inc(sem("R_dif"), 1)
                e.wait_ge(sem("R_exp"), 1)
                ch(ts(ga, dif, 1.0, None, ALU.add))
                ch(e.reciprocal(ga, ga))
                ch(tt(gb_, ga, dif, ALU.mult))
                for t in range(T):
                    ins = ts(gat[:, t, :], e1[:, t, :], ga[:, t, :], None, ALU.mult)
                ch(ins)
                for t in range(T):
                    ins = stt(gat[:, t, :], e2[:, t, :], gb_[:, t, :], gat[:, t, :], ALU.mult, ALU.add)
                ch(ins)
                e.wait_ge(sem("R_rank"), 1)
                ch(e.memset(rkm, -1.0))
                ch(stt(rkm[:, :, 0:NE], bank[2][:, 0:16].rearrange("p (t e) -> p t e", t=T), 1.0, mk,
                       ALU.add, ALU.mult))
                ch(ts(rkm[:, :, 0:NE], rkm[:, :, 0:NE], 1.0, None, ALU.subtract))
                ch(e.tensor_reduce(cnt, bank[2][:, 16:24], AX_X, ALU.max))
                e.tensor_copy(over[:], cnt).then_inc(sem("R_over"), 1)
                e.wait_ge(sem("R_over"), 1)

            e.wait_ge(sem("con_in"), 32)
            mixers(0)
            dense()
            mixers(1)
            norm(3, split=False)
            los(1, LAYER_UNITS + AHEAD, LAYER_UNITS + PAD)
            route()
            experts(0, MOE_AT, 2 * FB)
            with e.If(e.value_load(over[0:1, 0:1], min_val=0, max_val=S) > P):
                experts(1, AGAIN_AT, 2 * FB + NE * FB)


def lay_out(i):
    f = np.float32
    x = np.asarray(i["x"], f).reshape(S, D)

    def cols(a):
        return np.asarray(a, f).reshape(-1, P).T

    vec = np.zeros((P, LAYERS, NV), f)
    for L in range(LAYERS):
        def put(name, a):
            o, n = VEC[name]
            vec[:, L, o:o + n] = a

        def twice(a):
            return np.concatenate([a, a])[:, None]

        put("mix_g", cols(i["mix_norm_g"][L]))
        put("ffn_g", cols(i["ffn_norm_g"][L]))
        put("q_g", twice(i["attn_q_norm_g"][L]))
        z = np.zeros(HD, f)
        put("k_g0", np.concatenate([i["attn_k_norm_g"][L], z])[:, None])
        put("k_g1", np.concatenate([z, i["attn_k_norm_g"][L]])[:, None])
        put("conv_w", np.asarray(i["conv_w"][L], f).T.reshape(PAIRS, P, CW).transpose(1, 2, 0).reshape(P, -1))
        for name, key in (("conv_b", "conv_b"), ("conv_g", "conv_ln_g"), ("conv_lb", "conv_ln_b"), ("mu", "rwkv_mu"),
                          ("w0", "rwkv_w0"), ("a0", "rwkv_a0"), ("k_k", "rwkv_k_k"), ("k_a", "rwkv_k_a"),
                          ("r_k", "rwkv_r_k"), ("ln_g", "rwkv_ln_g"), ("ln_b", "rwkv_ln_b"), ("gb", "gla_gb")):
            put(name, cols(i[key][L]))
        put("gn_g", twice(i["gla_norm_g"][L]))
    lora = np.zeros((P, LAYERS, 3, GROUP), f)
    for L in range(LAYERS):
        lora[0:32, L, 0] = i["rwkv_w2"][L]
        lora[32:64, L, 1] = i["rwkv_a2"][L]
        lora[64:128, L, 2] = i["rwkv_g2"][L]
    gla2 = np.ascontiguousarray(np.asarray(i["gla_g2"], f).transpose(1, 0, 2))
    router = np.ascontiguousarray(np.asarray(i["moe_router"][0], f).reshape(KD, P, NE).transpose(1, 0, 2))

    wst = np.zeros((MAIN_UNITS, P, UC), f)

    def w_in(at, L):
        w = np.asarray(i["w_in"][L], f).reshape(KD, P, -1)
        for u, (c, n) in enumerate(Z_COLS):
            wst[at + u].reshape(P, KD, P)[:, :, :n] = w[:, :, c:c + n].transpose(1, 0, 2)

    def w_out(at, L):
        w = np.asarray(i["w_out"][L], f).reshape(KD, P, D)
        for u, k in enumerate((4, 5, 2, 3, 6, 7, 0, 1)):
            wst[at + u] = w[k]

    def gate_up(at, wg, wu, b):
        g = wg.reshape(KD, P, FF)[:, :, b * P:(b + 1) * P]
        u = wu.reshape(KD, P, FF)[:, :, b * P:(b + 1) * P]
        gu = np.concatenate([g, u], 2).transpose(1, 0, 2)
        wst[at] = gu[:, :4].reshape(P, UC)
        wst[at + 1] = gu[:, 4:].reshape(P, UC)

    for L in range(LAYERS):
        base = 0 if L == 0 else LAYER1_AT
        w_in(base, L)
        w_out(base + Z_UNITS, L)
    wg, wu, wd = (np.asarray(i[k][0], f) for k in ("ffn_wg", "ffn_wu", "ffn_wd"))
    for b in range(FB):
        gate_up(DENSE_AT + 3 * b, wg, wu, b)
        wst[DENSE_AT + 3 * b + 2] = wd[b * P:(b + 1) * P]
    for ex in range(NE):
        wg, wu, wd = (np.asarray(i[k][0][ex], f) for k in ("moe_wg", "moe_wu", "moe_wd"))
        at_ = MOE_AT + ex * F_UNITS
        for b in range(FB):
            gate_up(at_ + (0 if b == 0 else 2 + 3 * (b - 1)), wg, wu, b)
            wst[at_ + 2 + 3 * b + (2 if b < FB - 1 else 0)] = wd[b * P:(b + 1) * P]
    return {"x": x, "cons": constants(), "vecs": vec, "lora": lora, "gla2": gla2, "router": router,
            "relb": np.repeat(np.asarray(i["rel_bias"], f)[:, :, None], P, 2), "wst": wst}



def kernel(**inputs):
    import concourse.bacc as bacc
    from concourse.bass_utils import run_bass_kernel_spmd

    nc = bacc.Bacc("TRN2", target_bir_lowering=False, num_devices=1)
    arrays = lay_out({k: np.asarray(v) for k, v in inputs.items()})
    args = [nc.dram_tensor(f"in_{n}", a.shape, mybir.dt.from_np(a.dtype), kind="ExternalInput").ap()
            for n, a in arrays.items()]
    out = nc.dram_tensor("out_h", (S, D), F32, kind="ExternalOutput").ap()
    build(nc, *args, out)
    r = run_bass_kernel_spmd(nc, [{f"in_{n}": a for n, a in arrays.items()}], core_ids=[0])
    return r.results[0]["out_h"].reshape(1, S, D)
```
